# Optimizing a Trainium2 kernel written in Bass

```python
import math
import jax, jax.numpy as jnp
from jax import lax
import numpy as np

D_MODEL = 1024
BATCH = 1
SEQ = 128
DEPTH = 2
DEC_BATCH = 1
DEC_SEQ = 512
PAST_LEN = 128

GRID_W = 64
Q_BLOCK = 128
N_EVEN = (DEPTH + 1) // 2
N_ODD = DEPTH // 2
MIX_HALF = D_MODEL // 2
S5_WIDTH = MIX_HALF
S5_GROUP = 16
S5_GROUPS = S5_WIDTH // S5_GROUP
S5_STATE = 64
S5_DT_MIN = 0.001
S5_DT_MAX = 0.1
DIFF_HEADS = 4
DIFF_DK = MIX_HALF // (2 * DIFF_HEADS)
DIFF_DV = 2 * DIFF_DK
DIFF_QK = 2 * DIFF_HEADS * DIFF_DK
WIN_HEADS = 8
WIN_KV_HEADS = 2
WIN_GROUP = WIN_HEADS // WIN_KV_HEADS
WIN_DH = MIX_HALF // WIN_HEADS
WINDOW = 128
POOL_WINDOWS = (2, 4, 8, 16)
POOL_GROUP = MIX_HALF // len(POOL_WINDOWS)
PEER_HEADS = 8
PEER_NKEYS = 128
PEER_EXPERTS = PEER_NKEYS * PEER_NKEYS
PEER_TOPK = 16
PEER_DK = 256
PEER_DK_HALF = PEER_DK // 2
PEER_CHUNK = 128

EVEN_IN = S5_WIDTH + 2 * DIFF_QK + DIFF_HEADS * DIFF_DV
ODD_IN = WIN_HEADS * WIN_DH + 2 * WIN_KV_HEADS * WIN_DH + MIX_HALF
ROPE_BASE = 10000.0
EPS = 1e-6
NEG_INF = -1e30
F32 = jnp.float32

kernel_name = 'hybrid_diffusion_prefix_step'

def rms_norm(x, g):
    xf = x.astype(F32)
    y = xf * lax.rsqrt(jnp.mean(xf * xf, axis=-1, keepdims=True) + EPS)
    return (y * g.astype(F32)).astype(x.dtype)

def axial_rope_tables(n_rows, dim):
    q4 = dim // 4
    row = jnp.repeat(jnp.arange(n_rows), GRID_W).astype(F32)
    col = jnp.tile(jnp.arange(GRID_W), n_rows).astype(F32)
    freqs = ROPE_BASE ** (-jnp.arange(q4, dtype=F32) / q4)
    ang = jnp.stack([row[:, None] * freqs, col[:, None] * freqs], axis=1)
    return jnp.cos(ang), jnp.sin(ang)

def apply_axial_rope(x, cos, sin):
    shp = x.shape
    q4 = shp[-1] // 4
    nh = x.ndim - 3
    xr = x.astype(F32).reshape(shp[:-1] + (2, 2, q4))
    c = cos.reshape((1, shp[1]) + (1,) * nh + (2, q4))
    s = sin.reshape((1, shp[1]) + (1,) * nh + (2, q4))
    x1, x2 = xr[..., 0, :], xr[..., 1, :]
    out = jnp.stack([x1 * c - x2 * s, x2 * c + x1 * s], axis=-2)
    return out.reshape(shp).astype(x.dtype)

def sweep_blocks(fn, q):
    b, l = q.shape[:2]
    nb = l // Q_BLOCK
    qb = jnp.moveaxis(q.reshape((b, nb, Q_BLOCK) + q.shape[2:]), 1, 0)
    out = lax.map(lambda a: fn(a[0], a[1]), (qb, jnp.arange(nb)))
    o = jnp.moveaxis(out, 0, 1)
    return o.reshape((b, l) + o.shape[3:])

def _ssm_combine(e1, e2):
    a1, b1 = e1
    a2, b2 = e2
    return a1 * a2, a2 * b1 + b2

def s5_mixer(u, P, i, h0):
    bn, l, _ = u.shape
    uf = u.astype(F32)
    ug = uf.reshape(bn, l, S5_GROUPS, S5_GROUP).astype(jnp.complex64)
    y = P['s5_d'][i].astype(F32) * uf
    finals = []
    for d in range(2):
        rev = d == 1
        lam = lax.complex(P['s5_lam_re'][i, d].astype(F32), P['s5_lam_im'][i, d].astype(F32))
        step = jnp.exp(P['s5_log_step'][i, d].astype(F32))[:, None]
        a_bar = jnp.exp(lam * step)
        b_mat = lax.complex(P['s5_b_re'][i, d].astype(F32), P['s5_b_im'][i, d].astype(F32))
        b_bar = ((a_bar - 1.0) / lam)[..., None] * b_mat
        bu = jnp.einsum('blgc,gpc->blgp', ug, b_bar)
        a_cum, hs = lax.associative_scan(_ssm_combine, (jnp.broadcast_to(a_bar, bu.shape), bu),
                                         reverse=rev, axis=1)
        if h0 is not None:
            init = lax.complex(h0[:, d, 0].astype(F32), h0[:, d, 1].astype(F32))
            hs = hs + a_cum * init[:, None]
        else:
            hf = hs[:, 0] if rev else hs[:, -1]
            finals.append(jnp.stack([hf.real, hf.imag], axis=1))
        c_mat = lax.complex(P['s5_c_re'][i, d].astype(F32), P['s5_c_im'][i, d].astype(F32))
        y = y + jnp.einsum('blgp,gcp->blgc', hs, c_mat).real.reshape(bn, l, S5_WIDTH)
    g = jax.nn.gelu(y)
    out = (g * jax.nn.sigmoid(g @ P['s5_w_glu'][i].astype(F32))).astype(u.dtype)
    final = jnp.stack(finals, axis=1) if h0 is None else None
    return out, final

def diff_attention(q, k, v, lam):
    scale = DIFF_DK ** -0.5

    def block(qb, j):
        s = jnp.einsum('bqmhd,bkmhd->bmhqk', qb, k, preferred_element_type=F32) * scale
        p = jax.nn.softmax(s, axis=-1)
        a = p[:, 0] - lam * p[:, 1]
        return jnp.einsum('bhqk,bkhe->bqhe', a.astype(v.dtype), v)

    return sweep_blocks(block, q)

def sink_attention(q, k_ctx, v_ctx, sink, k_lat=None, v_lat=None):
    scale = WIN_DH ** -0.5
    l = q.shape[1]
    n_ctx = k_ctx.shape[1]
    local = k_lat is not None
    span = Q_BLOCK + 2 * WINDOW
    if local:
        pad = ((0, 0), (WINDOW, WINDOW), (0, 0), (0, 0))
        kp = jnp.pad(k_lat, pad)
        vp = jnp.pad(v_lat, pad)

    def block(qb, j):
        s = [jnp.einsum('bqngd,bknd->bngqk', qb, k_ctx, preferred_element_type=F32) * scale]
        if local:
            start = j * Q_BLOCK
            kl = lax.dynamic_slice_in_dim(kp, start, span, axis=1)
            vl = lax.dynamic_slice_in_dim(vp, start, span, axis=1)
            qpos = start + jnp.arange(Q_BLOCK)
            kpos = start - WINDOW + jnp.arange(span)
            ok = (jnp.abs(qpos[:, None] - kpos[None, :]) <= WINDOW) & (kpos >= 0)[None, :] & (kpos < l)[None, :]
            sl = jnp.einsum('bqngd,bknd->bngqk', qb, kl, preferred_element_type=F32) * scale
            s.append(jnp.where(ok, sl, NEG_INF))
        sk = jnp.broadcast_to(sink.astype(F32)[None, :, :, None, None], s[0].shape[:-1] + (1,))
        p = jax.nn.softmax(jnp.concatenate(s + [sk], axis=-1), axis=-1).astype(v_ctx.dtype)
        o = jnp.einsum('bngqk,bknd->bqngd', p[..., :n_ctx], v_ctx)
        if local:
            o = o + jnp.einsum('bngqk,bknd->bqngd', p[..., n_ctx:n_ctx + span], vl)
        return o

    return sweep_blocks(block, q)

def pool_mixer(u, w, scale):
    bn, l, _ = u.shape
    uf = u.astype(F32)
    cs = jnp.pad(jnp.cumsum(uf, axis=1), ((0, 0), (1, 0), (0, 0)))
    t = jnp.arange(l)
    parts = []
    for gi, wl in enumerate(POOL_WINDOWS):
        lo = jnp.clip(t - wl // 2, 0, l)
        hi = jnp.clip(t + wl - wl // 2, 0, l)
        csg = cs[:, :, gi * POOL_GROUP:(gi + 1) * POOL_GROUP]
        mean = (csg[:, hi] - csg[:, lo]) / (hi - lo).astype(F32)[None, :, None]
        parts.append(mean - uf[:, :, gi * POOL_GROUP:(gi + 1) * POOL_GROUP])
    pooled = jnp.stack(parts, axis=2)
    y = jnp.einsum('blgc,gcd->blgd', pooled, w.astype(F32)).reshape(bn, l, MIX_HALF) * scale.astype(F32)
    return y.astype(u.dtype)

def peer(h, w_q, sub_keys, u_tab, v_tab):
    bn, l, d = h.shape
    t = bn * l
    x = h.reshape(t, d)
    q = (x @ w_q).reshape(t, PEER_HEADS, 2, PEER_DK_HALF)
    s = jnp.einsum('thcd,hckd->thck', q, sub_keys, preferred_element_type=F32)
    s1, i1 = lax.top_k(s[:, :, 0], PEER_TOPK)
    s2, i2 = lax.top_k(s[:, :, 1], PEER_TOPK)
    cand = (s1[..., :, None] + s2[..., None, :]).reshape(t, PEER_HEADS, PEER_TOPK * PEER_TOPK)
    cidx = (i1[..., :, None] * PEER_NKEYS + i2[..., None, :]).reshape(t, PEER_HEADS, PEER_TOPK * PEER_TOPK)
    best, pos = lax.top_k(cand, PEER_TOPK)
    idx = jnp.take_along_axis(cidx, pos, axis=-1)
    gate = jax.nn.softmax(best, axis=-1)
    nc = t // PEER_CHUNK

    def chunk(args):
        xc, ic, gc = args
        a = jax.nn.gelu(jnp.einsum('td,thkd->thk', xc, jnp.take(u_tab, ic, axis=0), preferred_element_type=F32))
        return jnp.einsum('thk,thkd->td', (gc * a).astype(v_tab.dtype), jnp.take(v_tab, ic, axis=0))

    out = lax.map(chunk, (x.reshape(nc, PEER_CHUNK, d),
                          idx.reshape(nc, PEER_CHUNK, PEER_HEADS, PEER_TOPK),
                          gate.reshape(nc, PEER_CHUNK, PEER_HEADS, PEER_TOPK)))
    return out.reshape(bn, l, d).astype(h.dtype)

def even_mixer(h, i, lam_init, P, rope, cache):
    bn, l, _ = h.shape
    z = h @ P['even_w_in'][i]
    u, q, k, v = jnp.split(z, [S5_WIDTH, S5_WIDTH + DIFF_QK, S5_WIDTH + 2 * DIFF_QK], axis=-1)
    q = rms_norm(q.reshape(bn, l, 2, DIFF_HEADS, DIFF_DK), P['diff_q_norm'][i])
    k = rms_norm(k.reshape(bn, l, 2, DIFF_HEADS, DIFF_DK), P['diff_k_norm'][i])
    v = v.reshape(bn, l, DIFF_HEADS, DIFF_DV)
    lv = P['diff_lambda'][i].astype(F32)
    lam = jnp.exp(jnp.sum(lv[0] * lv[1])) - jnp.exp(jnp.sum(lv[2] * lv[3])) + lam_init
    if cache is None:
        k_all, v_all, h0 = k, v, None
    else:
        cos, sin = rope['diff']
        q = apply_axial_rope(q, cos, sin)
        k_all = jnp.concatenate([cache['diff_k'][:, i].astype(k.dtype), apply_axial_rope(k, cos, sin)], axis=1)
        v_all = jnp.concatenate([cache['diff_v'][:, i].astype(v.dtype), v], axis=1)
        h0 = cache['s5'][:, i]
    o_b = rms_norm(diff_attention(q, k_all, v_all, lam), P['diff_sub_norm'][i]) * (1.0 - lam_init)
    o_a, s5_final = s5_mixer(u, P, i, h0)
    out = jnp.concatenate([o_a, o_b.reshape(bn, l, MIX_HALF).astype(o_a.dtype)], axis=-1) @ P['even_w_out'][i]
    state = (k, v, s5_final) if cache is None else None
    return out, state

def odd_mixer(h, i, P, rope, cache):
    bn, l, _ = h.shape
    z = h @ P['odd_w_in'][i]
    nq = WIN_HEADS * WIN_DH
    nkv = WIN_KV_HEADS * WIN_DH
    q, k, v, u = jnp.split(z, [nq, nq + nkv, nq + 2 * nkv], axis=-1)
    q = rms_norm(q.reshape(bn, l, WIN_KV_HEADS, WIN_GROUP, WIN_DH), P['win_q_norm'][i])
    k = rms_norm(k.reshape(bn, l, WIN_KV_HEADS, WIN_DH), P['win_k_norm'][i])
    v = v.reshape(bn, l, WIN_KV_HEADS, WIN_DH)
    sink = P['win_sink'][i].reshape(WIN_KV_HEADS, WIN_GROUP)
    if cache is None:
        o_c = sink_attention(q, k, v, sink)
    else:
        cos, sin = rope['win']
        o_c = sink_attention(apply_axial_rope(q, cos, sin), cache['win_k'][:, i].astype(k.dtype),
                             cache['win_v'][:, i].astype(v.dtype), sink, apply_axial_rope(k, cos, sin), v)
    o_d = pool_mixer(u, P['pool_w'][i], P['pool_scale'][i])
    out = jnp.concatenate([o_c.reshape(bn, l, MIX_HALF).astype(o_d.dtype), o_d], axis=-1) @ P['odd_w_out'][i]
    state = (k, v) if cache is None else None
    return out, state

def trunk_layer(x, l, mod, P, rope, cache):
    shift_m, scale_m, gate_m, shift_f, scale_f, gate_f = jnp.split(mod, 6, axis=-1)
    h = rms_norm(x, P['norm_mix'][l]) * (1.0 + scale_m) + shift_m
    if l % 2 == 0:
        o, st = even_mixer(h, l // 2, 0.8 - 0.6 * math.exp(-0.3 * l), P, rope, cache)
    else:
        o, st = odd_mixer(h, l // 2, P, rope, cache)
    x = x + gate_m * o
    h = rms_norm(x, P['norm_ffn'][l]) * (1.0 + scale_f) + shift_f
    x = x + gate_f * peer(h, P['peer_w_q'][l], P['peer_sub_keys'][l], P['peer_u'][l], P['peer_v'][l])
    return x, st

def setup_inputs(seed: int = 0) -> dict:
    key = jax.random.key(seed)
    keys = jax.random.split(key, 64)
    cnt = [0]

    def nk():
        cnt[0] += 1
        return keys[cnt[0] - 1]

    def nrm(shape, s=1.0):
        return jax.random.normal(nk(), shape, F32) * s

    def gain(shape):
        return 1.0 + 0.02 * jax.random.normal(nk(), shape, F32)

    d = D_MODEL
    inp = {}
    inp['x_prompt'] = nrm((BATCH, SEQ, d))
    inp['x_sample'] = nrm((DEC_BATCH, DEC_SEQ, d))
    inp['cache_diff_k'] = nrm((DEC_BATCH, N_EVEN, PAST_LEN, 2, DIFF_HEADS, DIFF_DK))
    inp['cache_diff_v'] = nrm((DEC_BATCH, N_EVEN, PAST_LEN, DIFF_HEADS, DIFF_DV))
    inp['state_s5'] = nrm((DEC_BATCH, N_EVEN, 2, 2, S5_GROUPS, S5_STATE), 0.3)
    inp['cache_win_k'] = nrm((DEC_BATCH, N_ODD, PAST_LEN, WIN_KV_HEADS, WIN_DH))
    inp['cache_win_v'] = nrm((DEC_BATCH, N_ODD, PAST_LEN, WIN_KV_HEADS, WIN_DH))
    inp['c'] = nrm((DEC_BATCH, d))
    inp['c_ctx'] = nrm((d,))
    inp['ada_w'] = nrm((DEPTH, d, 6 * d), 0.5 * d ** -0.5)
    inp['ada_b'] = nrm((DEPTH, 6 * d), 0.02)
    inp['norm_mix'] = gain((DEPTH, d))
    inp['norm_ffn'] = gain((DEPTH, d))
    inp['even_w_in'] = nrm((N_EVEN, d, EVEN_IN), d ** -0.5)
    inp['even_w_out'] = nrm((N_EVEN, d, d), d ** -0.5)
    inp['s5_lam_re'] = -0.5 + nrm((N_EVEN, 2, S5_GROUPS, S5_STATE), 0.01)
    inp['s5_lam_im'] = jnp.pi * jnp.arange(S5_STATE, dtype=F32) + nrm((N_EVEN, 2, S5_GROUPS, S5_STATE), 0.01)
    inp['s5_log_step'] = jax.random.uniform(nk(), (N_EVEN, 2, S5_GROUPS), F32,
                                            minval=math.log(S5_DT_MIN), maxval=math.log(S5_DT_MAX))
    inp['s5_b_re'] = nrm((N_EVEN, 2, S5_GROUPS, S5_STATE, S5_GROUP), (2 * S5_GROUP) ** -0.5)
    inp['s5_b_im'] = nrm((N_EVEN, 2, S5_GROUPS, S5_STATE, S5_GROUP), (2 * S5_GROUP) ** -0.5)
    inp['s5_c_re'] = nrm((N_EVEN, 2, S5_GROUPS, S5_GROUP, S5_STATE), S5_STATE ** -0.5)
    inp['s5_c_im'] = nrm((N_EVEN, 2, S5_GROUPS, S5_GROUP, S5_STATE), S5_STATE ** -0.5)
    inp['s5_d'] = nrm((N_EVEN, S5_WIDTH))
    inp['s5_w_glu'] = nrm((N_EVEN, S5_WIDTH, S5_WIDTH), S5_WIDTH ** -0.5)
    inp['diff_q_norm'] = gain((N_EVEN, DIFF_DK))
    inp['diff_k_norm'] = gain((N_EVEN, DIFF_DK))
    inp['diff_lambda'] = nrm((N_EVEN, 4, DIFF_DK), 0.1)
    inp['diff_sub_norm'] = gain((N_EVEN, DIFF_DV))
    inp['odd_w_in'] = nrm((N_ODD, d, ODD_IN), d ** -0.5)
    inp['odd_w_out'] = nrm((N_ODD, d, d), d ** -0.5)
    inp['win_q_norm'] = gain((N_ODD, WIN_DH))
    inp['win_k_norm'] = gain((N_ODD, WIN_DH))
    inp['win_sink'] = nrm((N_ODD, WIN_HEADS), 0.5)
    inp['pool_w'] = nrm((N_ODD, len(POOL_WINDOWS), POOL_GROUP, POOL_GROUP), POOL_GROUP ** -0.5)
    inp['pool_scale'] = 1.0 + nrm((N_ODD, MIX_HALF), 0.1)
    inp['peer_w_q'] = nrm((DEPTH, d, PEER_HEADS * PEER_DK), d ** -0.5)
    inp['peer_sub_keys'] = nrm((DEPTH, PEER_HEADS, 2, PEER_NKEYS, PEER_DK_HALF), PEER_DK_HALF ** -0.5)
    inp['peer_u'] = nrm((DEPTH, PEER_EXPERTS, d), d ** -0.5)
    inp['peer_v'] = nrm((DEPTH, PEER_EXPERTS, d), PEER_HEADS ** -0.5)
    return inp

def reference(x_prompt, x_sample, cache_diff_k, cache_diff_v, state_s5, cache_win_k, cache_win_v, c,
              c_ctx, ada_w, ada_b, norm_mix, norm_ffn, even_w_in, even_w_out,
              s5_lam_re, s5_lam_im, s5_log_step, s5_b_re, s5_b_im, s5_c_re, s5_c_im, s5_d, s5_w_glu,
              diff_q_norm, diff_k_norm, diff_lambda, diff_sub_norm, odd_w_in, odd_w_out,
              win_q_norm, win_k_norm, win_sink, pool_w, pool_scale,
              peer_w_q, peer_sub_keys, peer_u, peer_v):
    P = dict(ada_w=ada_w, ada_b=ada_b, norm_mix=norm_mix, norm_ffn=norm_ffn,
             even_w_in=even_w_in, even_w_out=even_w_out,
             s5_lam_re=s5_lam_re, s5_lam_im=s5_lam_im, s5_log_step=s5_log_step,
             s5_b_re=s5_b_re, s5_b_im=s5_b_im, s5_c_re=s5_c_re, s5_c_im=s5_c_im,
             s5_d=s5_d, s5_w_glu=s5_w_glu,
             diff_q_norm=diff_q_norm, diff_k_norm=diff_k_norm, diff_lambda=diff_lambda,
             diff_sub_norm=diff_sub_norm, odd_w_in=odd_w_in, odd_w_out=odd_w_out,
             win_q_norm=win_q_norm, win_k_norm=win_k_norm, win_sink=win_sink,
             pool_w=pool_w, pool_scale=pool_scale,
             peer_w_q=peer_w_q, peer_sub_keys=peer_sub_keys, peer_u=peer_u, peer_v=peer_v)

    y = x_prompt
    diff_k, diff_v, s5_st, win_k, win_v = [], [], [], [], []
    for l in range(DEPTH):
        mod = (jax.nn.silu(c_ctx) @ ada_w[l] + ada_b[l])[None, None, :]
        y, st = trunk_layer(y, l, mod, P, None, None)
        if l % 2 == 0:
            diff_k.append(st[0])
            diff_v.append(st[1])
            s5_st.append(st[2])
        else:
            win_k.append(st[0])
            win_v.append(st[1])
    y_prompt = y

    n_lat = x_sample.shape[1]
    n_rows = n_lat // GRID_W
    rope = {'diff': axial_rope_tables(n_rows, DIFF_DK), 'win': axial_rope_tables(n_rows, WIN_DH)}
    cache = {'diff_k': cache_diff_k, 'diff_v': cache_diff_v, 's5': state_s5,
             'win_k': cache_win_k, 'win_v': cache_win_v}
    y = x_sample
    for l in range(DEPTH):
        mod = (jax.nn.silu(c) @ ada_w[l] + ada_b[l])[:, None, :]
        y, _ = trunk_layer(y, l, mod, P, rope, cache)
    y_sample = y

    new_diff_k = jnp.stack(diff_k, axis=1)
    new_diff_v = jnp.stack(diff_v, axis=1)
    new_s5 = jnp.stack(s5_st, axis=1)
    new_win_k = jnp.stack(win_k, axis=1)
    new_win_v = jnp.stack(win_v, axis=1)
    return (y_prompt, y_sample, new_diff_k, new_diff_v, new_s5, new_win_k, new_win_v)


_drawn_inputs = setup_inputs


def setup_inputs(seed=0):
    import zlib

    import numpy as np

    out = dict(_drawn_inputs(seed))
    spreads = {}
    factors = {'cache_win_k': 5.74,
     'cache_win_v': 4.752,
     'norm_mix': 2.907,
     'norm_ffn': 4.852,
     's5_lam_re': 4.266,
     's5_c_re': 2.724,
     's5_c_im': 2.789,
     'diff_q_norm': 8.0,
     'diff_k_norm': 2.876,
     'diff_lambda': 3.758,
     'diff_sub_norm': 8.0,
     'win_q_norm': 8.0,
     'win_k_norm': 3.556,
     'win_sink': 8.0,
     'pool_scale': 2.806}
    for name, (base, spread) in spreads.items():
        noise = np.random.default_rng([zlib.crc32(name.encode()), seed]).standard_normal(out[name].shape)
        drawn = base * np.exp(spread * noise) if base else spread * noise
        out[name] = __import__('jax').numpy.asarray(drawn.astype(out[name].dtype))
    for name, factor in factors.items():
        out[name] = (out[name] * factor).astype(out[name].dtype)
    return out
```

```python
import math
from contextlib import ExitStack

import numpy as np

import concourse.bass as bass
from concourse import mybir

F32 = mybir.dt.float32
BF16 = mybir.dt.bfloat16
U32 = mybir.dt.uint32
I32 = mybir.dt.int32
ALU = mybir.AluOpType
ACT = mybir.ActivationFunctionType
AX = mybir.AxisListType.X
AXY = mybir.AxisListType.XY

P = 128
D = 1024
KD = D // P
NT = 5
TOK = NT * P
HALF = 512
EPS = 1e-6
G = 32
CH = 16
S = 8
NCH = TOK // S
NCP = P // S
DK = 64
SCALE = DK ** -0.5
LAM_INIT = 0.8 - 0.6 * math.exp(0.0)
EVEN_IN = 2048
ODD_IN = 1280
EXPERTS = 16384
TOPK = 16
HEADS = 8
HK = HEADS * TOPK
RING = 16
ROUNDS = HK // RING
DIAGS = 4
TWO_PI_HI = 6.28125
TWO_PI_LO = 2 * math.pi - 6.28125
MAGIC = 12582912.0
POOL_WINDOWS = (2, 4, 8, 16)


class Count:

    def __init__(self, sem, step=1):
        self.sem, self.step, self.n = sem, step, 0

    def up(self):
        self.n += self.step
        return self.sem, self.step

    def now(self):
        return self.sem, self.n


def constants():
    ident = np.eye(P, dtype=np.float32)
    iota = np.tile(np.arange(16, dtype=np.float32), (P, 1))
    pos = np.arange(512)
    freqs = (np.float32(10000.0) ** (-np.arange(16, dtype=np.float32) / np.float32(16))).astype(np.float32)
    ang = np.stack([(pos // 64).astype(np.float32)[:, None] * freqs,
                    (pos % 64).astype(np.float32)[:, None] * freqs], axis=1)
    c, s = np.cos(ang).astype(np.float32), np.sin(ang).astype(np.float32)
    cos = np.stack([c, c], axis=2).reshape(4, P, DK).transpose(1, 0, 2).reshape(P, -1)
    sin = np.stack([-s, s], axis=2).reshape(4, P, DK).transpose(1, 0, 2).reshape(P, -1)
    q, k = np.arange(P)[:, None], np.arange(P)[None, :]
    before = np.where(k >= q, 0.0, -1e30).astype(np.float32)
    after = np.where(k <= q, 0.0, -1e30).astype(np.float32)
    small = np.concatenate([ident, iota, cos, sin, before, after], axis=1)

    pool = np.zeros((P, 6, 4, P), np.float32)
    for w, wl in enumerate(POOL_WINDOWS):
        def band(length, t0, s0):
            t = np.arange(t0, t0 + P)[None, :]
            src = np.arange(s0, s0 + P)[:, None]
            lo, hi = np.clip(t - wl // 2, 0, length), np.clip(t + wl - wl // 2, 0, length)
            return ((src >= lo) & (src < hi)) / (hi - lo).astype(np.float32) - (src == t)
        pool[:, 0, w] = band(128, 0, 0)
        pool[:, 1, w] = band(512, 0, 0)
        pool[:, 2, w] = band(512, 128, 128)
        pool[:, 3, w] = band(512, 384, 384)
        pool[:, 4, w] = band(512, 128, 0)
        pool[:, 5, w] = band(512, 128, 256)
    return np.ascontiguousarray(small, np.float32), np.ascontiguousarray(pool.reshape(P, -1), np.float32)


CONSTS = 128 + 16 + 256 + 256 + 128 + 128


def build(nc, I, O):
    with ExitStack() as ctx:
        def sem(name):
            return ctx.enter_context(nc.semaphore(name))

        def count(name, step=1):
            return Count(sem(name), step)

        SIZES = dict(X=5120, H=5120, MOD=7168, HT=5120, W=8192, MISC=3072, C=10240, D=5120, E=2048,
                     CONST=CONSTS, SMALL=600)
        arena = ctx.enter_context(nc.sbuf_tensor("arena", [P, sum(SIZES.values())], F32))
        at, off = {}, 0
        for name, size in SIZES.items():
            at[name] = off
            off += size

        def view(name, start, size, parts=P):
            return arena[0:parts, at[name] + start:at[name] + start + size]

        x = view("X", 0, 5120).rearrange("p (t d) -> p t d", t=NT)
        h = view("H", 0, 5120).rearrange("p (t d) -> p t d", t=NT)
        mod = view("MOD", 0, 6144).rearrange("p (c m d) -> p c m d", c=2, m=3)
        norm_row = view("MOD", 6144, 1024)
        hT = view("HT", 0, 5120).rearrange("p (k t) -> p k t", k=KD)
        wbuf = view("W", 0, 8192).rearrange("p (s n) -> p s n", s=2)
        ident = view("CONST", 0, 128)
        iota16 = view("CONST", 128, 16)
        rope_c = view("CONST", 144, 256).rearrange("p (t d) -> p t d", t=4)
        rope_s = view("CONST", 400, 256).rearrange("p (t d) -> p t d", t=4)
        mask_before = view("CONST", 656, 128)
        mask_after = view("CONST", 784, 128)
        ps = ctx.enter_context(nc.psum_tensor("ps", [P, 8, 512], F32))

        mod_dram = nc.dram_tensor("mod_rows", [2, 2, 6144], F32, kind="Internal").ap()
        bst_dram = nc.dram_tensor("s5_in", [2, P, G * P], F32, kind="Internal").ap()
        ca_dram = nc.dram_tensor("s5_out", [2, P, G * P], F32, kind="Internal").ap()
        kt_dram = nc.dram_tensor("s5_taps", [CH, G, 240], F32, kind="Internal").ap()

        block = ctx.enter_context(nc.Block())
        dve_did, act_did, pe_did, pool_did = count("dve_did"), count("act_did"), count("pe_did"), count("pool_did")
        full = [sem(f"bank_full{b}") for b in range(8)]
        free = [sem(f"bank_free{b}") for b in range(8)]
        w_in = [count(f"weights_in{s}", 16) for s in range(2)]
        dma_groups = []

        def group(name):
            dma_groups.append(count(f"{name}_{len(dma_groups)}", 16))
            return dma_groups[-1]
        w_last = [[], []]
        state = dict(items=0, w=0)

        def link(eng, did, ins):
            ins.then_inc(*did.up())
            eng.wait_ge(*did.now())

        def take(n):
            first = state["items"]
            state["items"] += n
            return first

        def bank(i):
            return ps[:, i % 8, :]

        def open_bank(pe, i):
            if i >= 8:
                pe.wait_ge(free[i % 8], i // 8)

        def filled(i):
            return full[i % 8], i // 8 + 1

        def emptied(i):
            return free[i % 8], i // 8 + 1

        def load_weights(src, shape_of, after=()):
            slot = state["w"] % 2
            state["w"] += 1
            dst = shape_of(wbuf[:, slot, :])

            @block.sync
            def _(sp):
                for mark in list(after) + w_last[slot]:
                    sp.wait_ge(*mark)
                sp.dma_start(dst, src).then_inc(*w_in[slot].up())
            return slot, dst, w_in[slot].now()

        def meet(engines="tvsgy"):
            marks = [c.now() for c in (dve_did, act_did, pe_did, pool_did, *dma_groups, w_in[0], w_in[1]) if c.n]
            n = state["items"]
            marks += [emptied(i) for i in range(max(0, n - 8), n)]

            def wait(eng):
                for mark in marks:
                    eng.wait_ge(*mark)
            if "t" in engines:
                @block.tensor
                def _(pe):
                    wait(pe)
            if "v" in engines:
                @block.vector
                def _(dve):
                    wait(dve)
            if "s" in engines:
                @block.scalar
                def _(act):
                    wait(act)
            if "g" in engines:
                @block.gpsimd
                def _(pool):
                    wait(pool)
            if "y" in engines:
                @block.sync
                def _(sp):
                    wait(sp)

        cond = view("SMALL", 0, 16).rearrange("p (j c) -> p j c", c=2)
        cond_sig = view("SMALL", 16, 16).rearrange("p (j c) -> p j c", c=2)
        ones2 = view("SMALL", 32, 2)
        a8_re = view("SMALL", 34, 32)
        a8_im = view("SMALL", 66, 32)
        a8_nim = view("SMALL", 98, 32)
        lam_col = view("SMALL", 130, 1)
        sink_col = view("SMALL", 131, 8)
        stat = view("SMALL", 139, 128)
        pscale_col = view("SMALL", 270, 4)
        stat2 = view("SMALL", 280, 128)
        zero_w = view("SMALL", 408, 64).bitcast(BF16)
        state0 = view("SMALL", 472, 64)
        lv_row = view("MISC", 0, 256)

        ld = group("loads_in")
        @block.sync
        def _(sp):
            sp.dma_start(view("CONST", 0, CONSTS), I["consts"]).then_inc(*ld.up())
            with nc.allow_non_contiguous_dma(reason="two conditioning columns"):
                sp.dma_start(cond[:, :, 0], I["c_ctx"].rearrange("(p j) -> p j", j=8)).then_inc(*ld.up())
                sp.dma_start(cond[:, :, 1], I["c"][0].rearrange("(p j) -> p j", j=8)).then_inc(*ld.up())
        cond_in = ld.now()
        ada_row = view("MOD", 0, 6144, 2)
        ada_bias = view("C", 0, 6144, 1)

        @block.scalar
        def _(act):
            act.wait_ge(*cond_in)
            nc.scalar.activation(cond_sig, cond, ACT.Sigmoid).then_inc(*act_did.up())
        sig_ready = act_did.now()

        @block.vector
        def _(dve):
            nc.vector.memset(ones2, 1.0).then_inc(*dve_did.up())
            nc.vector.memset(zero_w, 0.0).then_inc(*dve_did.up())
            dve.wait_ge(*sig_ready)
            nc.vector.tensor_tensor(cond, cond, cond_sig, ALU.mult).then_inc(*dve_did.up())
        cond_ready = dve_did.now()

        for l in range(2):
            store_before = st.now() if l else None

            ld = group("loads_in")
            @block.sync
            def _(sp):
                if l:
                    sp.wait_ge(*pe_did.now())
                sp.dma_start(ada_bias, I["ada_b"][l:l + 1, :]).then_inc(*ld.up())
            bias_in = ld.now()
            w_rows = I["ada_w"][l].rearrange("(p j) n -> p j n", j=8)
            for blk in range(12):
                slot, w, w_mark = load_weights(w_rows[:, :, blk * 512:(blk + 1) * 512],
                                               lambda a: a.rearrange("p (j n) -> p j n", j=8))
                i = take(1)
                w_last[slot] = [filled(i)]

                @block.tensor
                def _(pe):
                    open_bank(pe, i)
                    pe.wait_ge(*w_mark)
                    if blk == 0:
                        pe.wait_ge(*cond_ready)
                        pe.wait_ge(*bias_in)
                    for j in range(8):
                        nc.tensor.matmul(bank(i)[0:2, :], cond[:, j, :], w[:, j, :], start=(j == 0), stop=False)
                    nc.tensor.matmul(bank(i)[0:2, :], ones2[0:1, :], ada_bias[:, blk * 512:(blk + 1) * 512],
                                     start=False, stop=True).then_inc(*filled(i)[:1], 1)

                @block.scalar
                def _(act):
                    if blk == 0 and l:
                        act.wait_ge(*store_before)
                    act.wait_ge(*filled(i))
                    nc.scalar.copy(ada_row[:, blk * 512:(blk + 1) * 512], bank(i)[0:2, :]).then_inc(free[i % 8], 1)
            row_done = emptied(i)
            last_bank = filled(i)

            @block.tensor
            def _(pe):
                pe.wait_ge(*last_bank)
                pe.nop().then_inc(*pe_did.up())

            st = group("stores_out")
            @block.sync
            def _(sp):
                for b in range(8):
                    sp.wait_ge(*emptied(i - b))
                sp.dma_start(mod_dram[l], ada_row).then_inc(*st.up())

        def pv(start, size):
            return view("HT", start, size)
        lam = pv(0, 64).rearrange("p (r g) -> p r g", r=2)
        step = pv(64, 32)
        arg = pv(96, 64).rearrange("p (r g) -> p r g", r=2)
        mag = pv(160, 32)
        trig = pv(192, 64).rearrange("p (r g) -> p r g", r=2)
        den = pv(256, 32)
        fac = pv(288, 64).rearrange("p (r g) -> p r g", r=2)
        t32 = pv(352, 128).rearrange("p (n g) -> p n g", n=4)
        pw = pv(480, 576).rearrange("p (r k g) -> p r k g", r=2, k=9)
        pb = pv(1056, 512).rearrange("p (r s g) -> p r s g", r=2, s=8)
        pc = pv(1568, 512).rearrange("p (r s g) -> p r s g", r=2, s=8)
        braw = pv(2080, 1024).rearrange("p (r g c) -> p r g c", r=2, c=CH)
        bbar = pv(3104, 1024).rearrange("p (r g c) -> p r g c", r=2, c=CH)
        tmp = view("E", 0, 512).rearrange("p (g c) -> p g c", c=CH)
        tmp2 = view("E", 512, 512).rearrange("p (g c) -> p g c", c=CH)
        craw = view("E", 1024, 1024).rearrange("p (r g c) -> p r g c", r=2, c=CH)
        ncim = view("HT", 4128, 512).rearrange("p (g c) -> p g c", c=CH)
        BB = [view("C", 0, 4096).rearrange("p (g s c) -> p g s c", g=G, s=S),
              view("C", 4096, 4096).rearrange("p (g s c) -> p g s c", g=G, s=S)]
        CA = [arena[:, at["X"] + r * 4096:at["X"] + (r + 1) * 4096].rearrange("p (g s c) -> p g s c", g=G, s=S)
              for r in range(2)]

        ld = group("loads_in")
        @block.sync
        def _(sp):
            sp.dma_start(lam, I["s5_lam"]).then_inc(*ld.up())
            for d in range(2):
                sp.dma_start(step[64 * d:64 * d + 64, :], I["s5_log_step"][0, d:d + 1, :].to_broadcast([64, G])
                             ).then_inc(*ld.up())
            sp.dma_start(braw, I["s5_b"]).then_inc(*ld.up())
            sp.dma_start(craw, I["s5_c"]).then_inc(*ld.up())
            sp.dma_start(lv_row, I["diff_lambda"].rearrange("a b d -> a (b d)").to_broadcast([P, 256])).then_inc(*ld.up())
        s5_in = ld.now()

        @block.scalar
        def _(act):
            act.wait_ge(*s5_in)
            nc.scalar.activation(step, step, ACT.Exp).then_inc(*act_did.up())
        step_ready = act_did.now()

        @block.vector
        def _(dve):
            dve.wait_ge(*step_ready)
            v = nc.vector
            link(dve, dve_did, v.tensor_tensor(arg, lam, step.unsqueeze(1).to_broadcast([P, 2, G]), ALU.mult))
            link(dve, dve_did, v.tensor_scalar(t32[:, 0], arg[:, 1], 1 / (2 * math.pi), MAGIC, ALU.mult, ALU.add))
            link(dve, dve_did, v.tensor_scalar(t32[:, 0], t32[:, 0], -MAGIC, None, ALU.add))
            link(dve, dve_did, v.scalar_tensor_tensor(t32[:, 1], t32[:, 0], -TWO_PI_HI, arg[:, 1], ALU.mult, ALU.add))
            link(dve, dve_did, v.scalar_tensor_tensor(t32[:, 1], t32[:, 0], -TWO_PI_LO, t32[:, 1], ALU.mult, ALU.add))
            link(dve, dve_did, v.tensor_scalar(t32[:, 2], t32[:, 1], 0.0, None, ALU.is_gt))
            link(dve, dve_did, v.tensor_scalar(t32[:, 2], t32[:, 2], -2.0, 1.0, ALU.mult, ALU.add))
            link(dve, dve_did, v.tensor_tensor(t32[:, 2], t32[:, 1], t32[:, 2], ALU.mult))
            link(dve, dve_did, v.tensor_scalar(t32[:, 2], t32[:, 2], math.pi / 2, None, ALU.add))
            link(dve, dve_did, v.tensor_scalar(t32[:, 1], t32[:, 1], 3.1415925, -3.1415925, ALU.min, ALU.max))
        arg_ready = dve_did.now()

        @block.scalar
        def _(act):
            act.wait_ge(*arg_ready)
            nc.scalar.activation(mag, arg[:, 0], ACT.Exp).then_inc(*act_did.up())
            nc.scalar.activation(trig[:, 0], t32[:, 2], ACT.Sin).then_inc(*act_did.up())
            nc.scalar.activation(trig[:, 1], t32[:, 1], ACT.Sin).then_inc(*act_did.up())
        trig_ready = act_did.now()

        @block.vector
        def _(dve):
            v = nc.vector

            def L(ins):
                link(dve, dve_did, ins)

            def cmul(o_re, o_im, a_re, a_im, b_re, b_im, u, w):
                L(v.tensor_tensor(u, a_re, b_re, ALU.mult))
                L(v.tensor_tensor(w, a_im, b_im, ALU.mult))
                L(v.tensor_tensor(o_re, u, w, ALU.subtract))
                L(v.tensor_tensor(u, a_re, b_im, ALU.mult))
                L(v.tensor_tensor(w, a_im, b_re, ALU.mult))
                L(v.tensor_tensor(o_im, u, w, ALU.add))

            dve.wait_ge(*trig_ready)
            L(v.memset(pw[:, 0, 0], 1.0))
            L(v.memset(pw[:, 1, 0], 0.0))
            L(v.tensor_tensor(pw[:, 0, 1], mag, trig[:, 0], ALU.mult))
            L(v.tensor_tensor(pw[:, 1, 1], mag, trig[:, 1], ALU.mult))
            for k in range(2, 9):
                cmul(pw[:, 0, k], pw[:, 1, k], pw[:, 0, k - 1], pw[:, 1, k - 1], pw[:, 0, 1], pw[:, 1, 1],
                     t32[:, 0], t32[:, 1])
            L(v.tensor_copy(a8_re, pw[:, 0, 8]))
            L(v.tensor_copy(a8_im, pw[:, 1, 8]))
            L(v.tensor_scalar(a8_nim, pw[:, 1, 8], -1.0, None, ALU.mult))
            L(v.tensor_copy(pb[0:64], pw[0:64, :, 7::-1, :]))
            L(v.tensor_copy(pb[64:128], pw[64:128, :, 0:8, :]))
            L(v.tensor_copy(pc[0:64], pw[0:64, :, 1:9, :]))
            L(v.tensor_copy(pc[64:128], pw[64:128, :, 8:0:-1, :]))
            L(v.tensor_tensor(t32[:, 0], lam[:, 0], lam[:, 0], ALU.mult))
            L(v.tensor_tensor(t32[:, 1], lam[:, 1], lam[:, 1], ALU.mult))
            L(v.tensor_tensor(den, t32[:, 0], t32[:, 1], ALU.add))
            L(v.reciprocal(den, den))
            L(v.tensor_scalar(t32[:, 2], pw[:, 0, 1], -1.0, None, ALU.add))
            L(v.tensor_scalar(t32[:, 3], lam[:, 1], -1.0, None, ALU.mult))
            cmul(fac[:, 0], fac[:, 1], t32[:, 2], pw[:, 1, 1], lam[:, 0], t32[:, 3], t32[:, 0], t32[:, 1])
            L(v.tensor_tensor(fac, fac, den.unsqueeze(1).to_broadcast([P, 2, G]), ALU.mult))

            def over_c(a):
                return a.unsqueeze(2).to_broadcast([P, G, CH])
            cmul(bbar[:, 0], bbar[:, 1], braw[:, 0], braw[:, 1], over_c(fac[:, 0]), over_c(fac[:, 1]), tmp, tmp2)
            L(v.tensor_scalar(ncim, craw[:, 1], -1.0, None, ALU.mult))
            for s in range(S):
                cmul(BB[0][:, :, s, :], BB[1][:, :, s, :], bbar[:, 0], bbar[:, 1],
                     over_c(pb[:, 0, s]), over_c(pb[:, 1, s]), tmp, tmp2)
            for s in range(S):
                cmul(CA[0][:, :, s, :], CA[1][:, :, s, :], craw[:, 0], craw[:, 1],
                     over_c(pc[:, 0, s]), over_c(pc[:, 1, s]), tmp, tmp2)
                L(v.tensor_scalar(CA[1][:, :, s, :], CA[1][:, :, s, :], -1.0, None, ALU.mult))
            L(v.tensor_tensor(lv_row[:, 0:64], lv_row[:, 0:64], lv_row[:, 64:128], ALU.mult))
            L(v.tensor_tensor(lv_row[:, 128:192], lv_row[:, 128:192], lv_row[:, 192:256], ALU.mult))
            L(v.tensor_reduce(stat[:, 0:1], lv_row[:, 0:64], AX, ALU.add))
            L(v.tensor_reduce(stat[:, 1:2], lv_row[:, 128:192], AX, ALU.add))
        tables_ready = dve_did.now()

        @block.scalar
        def _(act):
            act.wait_ge(*tables_ready)
            nc.scalar.activation(stat[:, 0:2], stat[:, 0:2], ACT.Exp).then_inc(*act_did.up())
        lam_exp = act_did.now()

        @block.vector
        def _(dve):
            dve.wait_ge(*lam_exp)
            link(dve, dve_did, nc.vector.tensor_tensor(lam_col, stat[:, 0:1], stat[:, 1:2], ALU.subtract))
            link(dve, dve_did, nc.vector.tensor_scalar(lam_col, lam_col, LAM_INIT, None, ALU.add))

        bst = view("D", 0, 4096).rearrange("p (g m) -> p g m", g=G)
        meet("t")
        for r in range(2):
            i0 = take(8)
            out_before = st.now()

            @block.tensor
            def _(pe):
                for n in range(8):
                    open_bank(pe, i0 + n)
                    for q in range(4):
                        g = 4 * n + q
                        ins = nc.tensor.transpose(bank(i0 + n)[:, q * P:(q + 1) * P],
                                                  BB[r][:, g].rearrange("p s c -> p (s c)"), ident)
                    ins.then_inc(full[(i0 + n) % 8], 1)

            @block.scalar
            def _(act):
                if r:
                    act.wait_ge(*out_before)
                for n in range(8):
                    act.wait_ge(*filled(i0 + n))
                    nc.scalar.copy(bst[:, 4 * n:4 * n + 4, :].rearrange("p g m -> p (g m)"), bank(i0 + n)).then_inc(free[(i0 + n) % 8], 1)

            st = group("stores_out")
            @block.sync
            def _(sp):
                for n in range(8):
                    sp.wait_ge(*emptied(i0 + n))
                sp.dma_start(bst_dram[r], bst.rearrange("p g m -> p (g m)")).then_inc(*st.up())
                if r == 0:
                    sp.wait_ge(*tables_ready)
                sp.dma_start(ca_dram[r], CA[r].rearrange("p g s c -> p (g s c)")).then_inc(*st.up())

        taps = view("C", 0, G * 240, CH).rearrange("p (g o) -> p g o", g=G)
        i0 = take(17)
        lo, hi = slice(0, 64), slice(64, 128)

        def ca(r, rows, g, j0):
            return CA[r][rows, g, j0:j0 + 7, :].rearrange("p s c -> p (s c)")

        @block.tensor
        def _(pe):
            for n in range(16):
                rows, j0 = (lo, 0) if n < 8 else (hi, 1)
                open_bank(pe, i0 + n)
                for q in range(4):
                    g = 4 * (n % 8) + q
                    for r in range(2):
                        ins = nc.tensor.matmul(bank(i0 + n)[0:CH, 112 * q:112 * q + 112], bbar[rows, r, g], ca(r, rows, g, j0),
                                               start=(r == 0), stop=(r == 1))
                ins.then_inc(full[(i0 + n) % 8], 1)
            open_bank(pe, i0 + 16)
            for g in range(G):
                o = bank(i0 + 16)[0:CH, CH * g:CH * g + CH]
                nc.tensor.matmul(o, bbar[:, 0, g], craw[:, 0, g], start=True, stop=False)
                ins = nc.tensor.matmul(o, bbar[:, 1, g], ncim[:, g], start=False, stop=True)
            ins.then_inc(full[(i0 + 16) % 8], 1)

        @block.scalar
        def _(act):
            for n in range(17):
                act.wait_ge(*filled(i0 + n))
                g, o = 4 * (n % 8), 128 if n < 8 else 0
                dst = taps[:, g:g + 4, o:o + 112] if n < 16 else taps[:, :, 112:128]
                src = bank(i0 + n)[0:CH, 0:448].rearrange("p (g o) -> p g o", g=4) if n < 16 else \
                    bank(i0 + n)[0:CH, :].rearrange("p (g o) -> p g o", g=G)
                nc.scalar.copy(dst, src).then_inc(free[(i0 + n) % 8], 1)

        st = group("stores_out")
        @block.sync
        def _(sp):
            for n in range(9, 17):
                sp.wait_ge(*emptied(i0 + n))
            sp.dma_start(kt_dram, taps).then_inc(*st.up())
        meet()

        ld = group("loads_in")
        @block.sync
        def _(sp):
            sp.dma_start(x[:, 0, :], I["x_prompt"][0]).then_inc(*ld.up())
            sp.dma_start(x[:, 1:5, :], I["x_sample"][0].rearrange("(t p) d -> p t d", p=P)).then_inc(*ld.up())

        def modulate(l, which, norm):
            ld = group("loads_in")
            x_ready = dve_did.now()

            @block.sync
            def _(sp):
                sp.wait_ge(*x_ready)
                for c in range(2):
                    sp.dma_start(mod[:, c].rearrange("p m d -> p (m d)"),
                                 mod_dram[l, c:c + 1, which * 3072:(which + 1) * 3072].to_broadcast([P, 3072])
                                 ).then_inc(*ld.up())
                sp.dma_start(norm_row, norm[l:l + 1, :].to_broadcast([P, D])).then_inc(*ld.up())
            mods_in = ld.now()

            @block.scalar
            def _(act):
                act.wait_ge(*mods_in)
                act.wait_ge(*x_ready)
                for t in range(NT):
                    nc.scalar.activation(h[:, t], x[:, t], ACT.Square, accum_out=stat[:, t:t + 1]).then_inc(*act_did.up())
            squares = act_did.now()

            @block.vector
            def _(dve):
                dve.wait_ge(*mods_in)
                for c in range(2):
                    nc.vector.scalar_tensor_tensor(mod[:, c, 1], mod[:, c, 1], 1.0, norm_row, ALU.add, ALU.mult).then_inc(*dve_did.up())
                dve.wait_ge(*squares)
                link(dve, dve_did, nc.vector.tensor_scalar(stat[:, 0:NT], stat[:, 0:NT], 1.0 / D, EPS, ALU.mult, ALU.add))
            var_ready = dve_did.now()

            @block.scalar
            def _(act):
                act.wait_ge(*var_ready)
                nc.scalar.activation(stat[:, 8:8 + NT], stat[:, 0:NT], ACT.Sqrt).then_inc(*act_did.up())
            std_ready = act_did.now()
            tile_ready = []

            @block.vector
            def _(dve):
                dve.wait_ge(*std_ready)
                link(dve, dve_did, nc.vector.reciprocal(stat[:, 16:16 + NT], stat[:, 8:8 + NT]))
                for t in range(NT):
                    c = min(t, 1)
                    link(dve, dve_did, nc.vector.scalar_tensor_tensor(h[:, t], x[:, t], stat[:, 16 + t:17 + t], mod[:, c, 1], ALU.mult, ALU.mult))
                    nc.vector.tensor_tensor(h[:, t], h[:, t], mod[:, c, 0], ALU.add).then_inc(*dve_did.up())
                    tile_ready.append(dve_did.now())
            i0 = take(2 * NT)

            @block.tensor
            def _(pe):
                for t in range(NT):
                    pe.wait_ge(*tile_ready[t])
                    for b in range(2):
                        i = i0 + 2 * t + b
                        open_bank(pe, i)
                        for q in range(4):
                            ins = nc.tensor.transpose(bank(i)[:, q * P:(q + 1) * P], h[:, t, (4 * b + q) * P:(4 * b + q + 1) * P], ident)
                        ins.then_inc(full[i % 8], 1)

            @block.scalar
            def _(act):
                for t in range(NT):
                    for b in range(2):
                        i = i0 + 2 * t + b
                        act.wait_ge(*filled(i))
                        nc.scalar.copy(hT[:, 4 * b:4 * b + 4, t * P:(t + 1) * P],
                                       bank(i).rearrange("p (q t) -> p q t", q=4)).then_inc(free[i % 8], 1)
            return [emptied(i0 + n) for n in range(2 * NT)][-8:]

        def project(w_in_dram, col0, ncols, dst, ready):
            slot, w, w_mark = load_weights(w_in_dram.rearrange("(k p) n -> p k n", p=P)[:, :, col0:col0 + ncols],
                                           lambda a: a[:, 0:8 * ncols].rearrange("p (k n) -> p k n", k=KD))
            i0 = take(NT)
            w_last[slot] = [filled(i0 + NT - 1)]

            @block.tensor
            def _(pe):
                for m in ready:
                    pe.wait_ge(*m)
                pe.wait_ge(*w_mark)
                for t in range(NT):
                    open_bank(pe, i0 + t)
                    for k in range(KD):
                        ins = nc.tensor.matmul(bank(i0 + t)[:, 0:ncols], hT[:, k, t * P:(t + 1) * P], w[:, k, :],
                                               start=(k == 0), stop=(k == KD - 1))
                    ins.then_inc(full[(i0 + t) % 8], 1)

            @block.scalar
            def _(act):
                for t in range(NT):
                    act.wait_ge(*filled(i0 + t))
                    nc.scalar.copy(dst(t), bank(i0 + t)[:, 0:ncols]).then_inc(free[(i0 + t) % 8], 1)
            return [emptied(i0 + t) for t in range(NT)]

        def transposes(srcs, dst_of, ready, rows=P):
            i0 = take(len(srcs))

            @block.tensor
            def _(pe):
                for m in ready:
                    pe.wait_ge(*m)
                for n, group in enumerate(srcs):
                    open_bank(pe, i0 + n)
                    for q, src in enumerate(group):
                        k = src.shape[0]
                        ins = nc.tensor.transpose(bank(i0 + n)[:, q * P:q * P + k], src, ident[0:k, 0:k])
                    ins.then_inc(full[(i0 + n) % 8], 1)

            @block.scalar
            def _(act):
                for n, group in enumerate(srcs):
                    k = group[0].shape[0]
                    act.wait_ge(*filled(i0 + n))
                    src = bank(i0 + n)[:, 0:len(group) * P].rearrange("p (q t) -> p q t", t=P)[:, :, 0:k]
                    nc.scalar.copy(dst_of(n), src).then_inc(free[(i0 + n) % 8], 1)
            return [emptied(i0 + n) for n in range(len(srcs))][-8:]

        def qk_norm_rope(z, width, gain, tmp_sq, ready):
            g = width // DK
            for t in range(NT):
                zt = z(t)[:, 0:width].rearrange("p (g d) -> p g d", d=DK)
                sq = tmp_sq[:, 0:width].rearrange("p (g d) -> p g d", d=DK)

                @block.vector
                def _(dve):
                    for m in ready:
                        dve.wait_ge(*m)
                    link(dve, dve_did, nc.vector.tensor_tensor(sq, zt, zt, ALU.mult))
                    link(dve, dve_did, nc.vector.tensor_reduce(stat[:, 0:g], sq, AX, ALU.add))
                    link(dve, dve_did, nc.vector.tensor_scalar(stat[:, 0:g], stat[:, 0:g], 1.0 / DK, EPS, ALU.mult, ALU.add))
                var_ready = dve_did.now()

                @block.scalar
                def _(act):
                    act.wait_ge(*var_ready)
                    nc.scalar.activation(stat[:, 16:16 + g], stat[:, 0:g], ACT.Sqrt).then_inc(*act_did.up())
                std_ready = act_did.now()

                @block.vector
                def _(dve):
                    dve.wait_ge(*std_ready)
                    link(dve, dve_did, nc.vector.reciprocal(stat[:, 32:32 + g], stat[:, 16:16 + g]))
                    link(dve, dve_did, nc.vector.tensor_tensor(zt, zt, stat[:, 32:32 + g].unsqueeze(2).to_broadcast([P, g, DK]), ALU.mult))
                    link(dve, dve_did, nc.vector.tensor_tensor(z(t)[:, 0:width], z(t)[:, 0:width], gain[:, 0:width], ALU.mult))
                    if t:
                        z4 = z(t)[:, 0:width].rearrange("p (g a b) -> p g a b", a=2, b=32)
                        s4 = tmp_sq[:, 0:width].rearrange("p (g a b) -> p g a b", a=2, b=32)
                        c_t = rope_c[:, t - 1].unsqueeze(1).to_broadcast([P, g, DK])
                        s_t = rope_s[:, t - 1].rearrange("p (a b) -> p a b", a=2)
                        for half in range(2):
                            o, i = 16 * half, 16 - 16 * half
                            nc.vector.tensor_tensor(s4[:, :, :, o:o + 16], z4[:, :, :, i:i + 16],
                                                    s_t[:, :, o:o + 16].unsqueeze(1).to_broadcast([P, g, 2, 16]),
                                                    ALU.mult).then_inc(*dve_did.up())
                        dve.wait_ge(*dve_did.now())
                        link(dve, dve_did, nc.vector.tensor_tensor(zt, zt, c_t, ALU.mult))
                        link(dve, dve_did, nc.vector.tensor_tensor(zt, zt, sq, ALU.add))
            return [dve_did.now()]

        def out_project(w_dram, cat, ready):
            for n in range(2):
                slot, w, w_mark = load_weights(w_dram.rearrange("(k p) n -> p k n", p=P)[:, :, n * 512:(n + 1) * 512],
                                               lambda a: a.rearrange("p (k n) -> p k n", k=KD))
                i0 = take(NT)
                w_last[slot] = [filled(i0 + NT - 1)]

                @block.tensor
                def _(pe):
                    for m in ready:
                        pe.wait_ge(*m)
                    pe.wait_ge(*w_mark)
                    for t in range(NT):
                        open_bank(pe, i0 + t)
                        for k in range(KD):
                            ins = nc.tensor.matmul(bank(i0 + t), cat(k)[:, t * P:(t + 1) * P], w[:, k, :],
                                                   start=(k == 0), stop=(k == KD - 1))
                        ins.then_inc(full[(i0 + t) % 8], 1)

                @block.vector
                def _(dve):
                    for t in range(NT):
                        dve.wait_ge(*filled(i0 + t))
                        add_gated(dve, t, n, bank(i0 + t), free[(i0 + t) % 8], view("E", 0, 512))

        def add_gated(dve, t, n, src, src_free, tmp512):
            cols = slice(n * 512, (n + 1) * 512)
            nc.vector.tensor_tensor(tmp512, src, mod[:, min(t, 1), 2, cols], ALU.mult).then_inc(src_free, 1)
            link(dve, dve_did, nc.vector.memset(stat2[:, 127:128], 0.0))
            link(dve, dve_did, nc.vector.tensor_tensor(x[:, t, cols], x[:, t, cols], tmp512, ALU.add))

        hT_ready = modulate(0, 0, I["norm_mix"])

        u_c = view("C", 0, 4096, NCH).rearrange("p (g s c) -> p g s c", g=G, s=S)
        slot, w, w_mark = load_weights(I["even_w_in"][0].rearrange("(k p) n -> p k n", p=P)[:, :, 0:512],
                                       lambda a: a.rearrange("p (k n) -> p k n", k=KD))
        i0 = take(S)
        w_last[slot] = [filled(i0 + S - 1)]

        @block.tensor
        def _(pe):
            for m in hT_ready:
                pe.wait_ge(*m)
            pe.wait_ge(*w_mark)
            for s in range(S):
                open_bank(pe, i0 + s)
                for k in range(KD):
                    ins = nc.tensor.matmul(bank(i0 + s)[0:NCH, :], hT[:, k, s:TOK:S], w[:, k, :],
                                           start=(k == 0), stop=(k == KD - 1))
                ins.then_inc(full[(i0 + s) % 8], 1)

        @block.scalar
        def _(act):
            for s in range(S):
                act.wait_ge(*filled(i0 + s))
                nc.scalar.copy(u_c[:, :, s, :], bank(i0 + s)[0:NCH, :].rearrange("p (g c) -> p g c", g=G)).then_inc(free[(i0 + s) % 8], 1)
        u_ready = [emptied(i0 + s) for s in range(S)]

        xg = view("C", 4096, G * NCH).rearrange("p (g n) -> p g n", g=G)
        i0 = take(6)

        @block.tensor
        def _(pe):
            for m in u_ready:
                pe.wait_ge(*m)
            for b in range(6):
                open_bank(pe, i0 + b)
                for q in range(min(6, G - 6 * b)):
                    g = 6 * b + q
                    ins = nc.tensor.transpose(bank(i0 + b)[:, q * NCH:(q + 1) * NCH], u_c[:, g].rearrange("p s c -> p (s c)"),
                                              ident[0:NCH, 0:NCH])
                ins.then_inc(full[(i0 + b) % 8], 1)

        @block.scalar
        def _(act):
            for b in range(6):
                k = min(6, G - 6 * b)
                act.wait_ge(*filled(i0 + b))
                nc.scalar.copy(xg[:, 6 * b:6 * b + k, :].rearrange("p g n -> p (g n)"), bank(i0 + b)[:, 0:k * NCH]
                               ).then_inc(free[(i0 + b) % 8], 1)
        xg_ready = [emptied(i0 + b) for b in range(6)]

        hs = view("D", 0, 5120).rearrange("p (r g k) -> p r g k", r=2, g=G)
        for hf in range(2):
            slot, w, w_mark = load_weights(bst_dram.rearrange("r p (g m) -> p r g m", g=G)[:, :, 16 * hf:16 * hf + 16, :],
                                           lambda a: a.rearrange("p (r g m) -> p r g m", r=2, g=16))
            i0 = take(8)
            w_last[slot] = [filled(i0 + 7)]

            @block.tensor
            def _(pe):
                for m in xg_ready:
                    pe.wait_ge(*m)
                pe.wait_ge(*w_mark)
                for b in range(8):
                    open_bank(pe, i0 + b)
                    for q in range(4):
                        r, g = b // 4, 4 * (b % 4) + q
                        ins = nc.tensor.matmul(bank(i0 + b)[:, q * NCH:(q + 1) * NCH], w[:, r, g, :], xg[:, 16 * hf + g, :],
                                               start=True, stop=True)
                    ins.then_inc(full[(i0 + b) % 8], 1)

            @block.scalar
            def _(act):
                for b in range(8):
                    r, g = b // 4, 16 * hf + 4 * (b % 4)
                    src = bank(i0 + b)[:, 0:4 * NCH].rearrange("p (q n) -> p q n", q=4)
                    act.wait_ge(*filled(i0 + b))
                    nc.scalar.copy(hs[0:64, r, g:g + 4, :], src[0:64])
                    nc.scalar.copy(hs[64:128, r, g:g + 4, 0:NCP], src[64:128, :, NCP - 1::-1])
                    nc.scalar.copy(hs[64:128, r, g:g + 4, NCP:NCH], src[64:128, :, NCH - 1:NCP - 1:-1]
                                   ).then_inc(free[(i0 + b) % 8], 1)
            if hf == 0:
                hs_ready = [emptied(i0 + b) for b in range(8)]
        hs_ready += [emptied(i0 + b) for b in range(8)]

        s5_d_row = view("MOD", 6144, 512, NCH)
        h0 = state0.rearrange("p (r g) -> p r g", r=2)

        ld = group("loads_in")
        @block.sync
        def _(sp):
            sp.wait_ge(*dve_did.now())
            sp.dma_start(h0, I["state_s5"]).then_inc(*ld.up())
            sp.dma_start(s5_d_row, I["s5_d"].to_broadcast([NCH, 512])).then_inc(*ld.up())
        h0_in = ld.now()

        s_scan = sem("scan_steps")
        hop = view("E", 0, 128).rearrange("p (n r g) -> p n r g", n=2, r=2)
        scans = [0]

        def scan_step(dve, before, cur, value):
            a_re = a8_re.unsqueeze(1).to_broadcast([P, 2, G])
            nc.vector.tensor_tensor(hop[:, 0], before, a_re, ALU.mult)
            nc.vector.tensor_tensor(hop[:, 1, 0], before[:, 1], a8_nim, ALU.mult)
            nc.vector.tensor_tensor(hop[:, 1, 1], before[:, 0], a8_im, ALU.mult).then_inc(s_scan, 1)
            dve.wait_ge(s_scan, value + 1)
            nc.vector.tensor_tensor(hop[:, 0], hop[:, 0], hop[:, 1], ALU.add).then_inc(s_scan, 1)
            dve.wait_ge(s_scan, value + 2)
            nc.vector.tensor_tensor(cur, cur, hop[:, 0], ALU.add).then_inc(s_scan, 1)
            dve.wait_ge(s_scan, value + 3)

        @block.vector
        def _(dve):
            dve.wait_ge(*h0_in)
            for m in hs_ready:
                dve.wait_ge(*m)
            with dve.Fori(1, NCP) as k:
                scan_step(dve, hs[:, :, :, bass.ds(k - 1, 1)].rearrange("p r g k -> p r (g k)"),
                          hs[:, :, :, bass.ds(k, 1)].rearrange("p r g k -> p r (g k)"), 3 * (k - 1))
            scan_step(dve, h0, hs[:, :, :, NCP], 3 * (NCP - 1))
            with dve.Fori(NCP + 1, NCH) as k:
                scan_step(dve, hs[:, :, :, bass.ds(k - 1, 1)].rearrange("p r g k -> p r (g k)"),
                          hs[:, :, :, bass.ds(k, 1)].rearrange("p r g k -> p r (g k)"), 3 * (k - 1))
        scan_done = (s_scan, 3 * (NCH - 1))

        fin_in = view("E", 128, 64)
        fin_out = view("E", 256, 128, 64)

        @block.vector
        def _(dve):
            link(dve, dve_did, nc.vector.tensor_copy(fin_in.rearrange("p (r g) -> p r g", r=2), hs[:, :, :, NCP - 1]))
        fin_ready = dve_did.now()
        i0 = take(1)

        @block.tensor
        def _(pe):
            open_bank(pe, i0)
            pe.wait_ge(*fin_ready)
            nc.tensor.transpose(bank(i0)[0:64, 0:P], fin_in, ident).then_inc(full[i0 % 8], 1)

        @block.scalar
        def _(act):
            act.wait_ge(*filled(i0))
            nc.scalar.copy(fin_out, bank(i0)[0:64, 0:P]).then_inc(free[i0 % 8], 1)

        st = group("stores_out")
        @block.sync
        def _(sp):
            sp.wait_ge(*emptied(i0))
            for d in range(2):
                sp.dma_start(O["new_s5"][0, 0, d].rearrange("r g p -> (r g) p"), fin_out[:, 64 * d:64 * d + 64]).then_inc(*st.up())

        hin = view("H", 0, 5120).rearrange("p (r g n) -> p r g n", r=2, g=G)

        @block.scalar
        def _(act):
            act.wait_ge(*scan_done)
            nc.scalar.copy(hin[0:64, :, :, 1:NCP], hs[0:64, :, :, 0:NCP - 1])
            nc.scalar.copy(hin[0:64, :, :, NCP + 1:NCH], hs[0:64, :, :, NCP:NCH - 1])
            nc.scalar.copy(hin[64:128, :, :, 0:NCP - 1], hs[64:128, :, :, NCP - 2::-1])
            nc.scalar.copy(hin[64:128, :, :, NCP:NCH - 1], hs[64:128, :, :, NCH - 2:NCP - 1:-1])
            nc.scalar.copy(hin[0:64, :, :, NCP], h0[0:64])
            nc.scalar.copy(hin[64:128, :, :, NCH - 1], h0[64:128])
            nc.scalar.activation(hin[0:64, :, :, 0], h0[0:64], ACT.Copy, scale=0.0)
            nc.scalar.activation(hin[64:128, :, :, NCP - 1], h0[64:128], ACT.Copy, scale=0.0).then_inc(*act_did.up())
        hin_ready = act_did.now()

        toep = wbuf[:, state["w"] % 2, :].rearrange("p (g m) -> p g m", g=G)
        t_slot = state["w"] % 2
        state["w"] += 1

        @block.sync
        def _(sp):
            for m in w_last[t_slot]:
                sp.wait_ge(*m)
            for s in range(S):
                sp.dma_start(toep[CH * s:CH * s + CH, :, :], kt_dram[:, :, (7 - s) * CH:(7 - s) * CH + P]).then_inc(*w_in[t_slot].up())
        toep_in = w_in[t_slot].now()

        i0 = take(8)

        @block.vector
        def _(dve):
            link(dve, dve_did, nc.vector.tensor_tensor(u_c, u_c, s5_d_row.rearrange("p (g c) -> p g c", g=G).unsqueeze(2).to_broadcast([NCH, G, S, CH]), ALU.mult))

        @block.tensor
        def _(pe):
            pe.wait_ge(*toep_in)
            for b in range(8):
                open_bank(pe, i0 + b)
                for q in range(4):
                    g = 4 * b + q
                    ins = nc.tensor.matmul(bank(i0 + b)[0:NCH, q * P:(q + 1) * P], xg[:, g, :], toep[:, g, :], start=True, stop=True)
                ins.then_inc(full[(i0 + b) % 8], 1)
        w_last[t_slot] = [filled(i0 + 7)]

        def add_y(i0, nb, g0):
            @block.vector
            def _(dve):
                for b in range(nb):
                    g = g0 + 4 * b
                    dst = u_c[:, g:g + 4].rearrange("p g s c -> p (g s c)")
                    src = bank(i0 + b)[0:NCH, :]
                    dve.wait_ge(*filled(i0 + b))
                    nc.vector.tensor_tensor(dst, dst, src, ALU.add).then_inc(free[(i0 + b) % 8], 1)
        add_y(i0, 8, 0)
        for hf in range(2):
            slot, w, w_mark = load_weights(ca_dram.rearrange("r p (g m) -> p r g m", g=G)[:, :, 16 * hf:16 * hf + 16, :],
                                           lambda a: a.rearrange("p (r g m) -> p r g m", r=2, g=16))
            i0 = take(4)
            w_last[slot] = [filled(i0 + 3)]

            @block.tensor
            def _(pe):
                pe.wait_ge(*hin_ready)
                pe.wait_ge(*w_mark)
                for b in range(4):
                    open_bank(pe, i0 + b)
                    for q in range(4):
                        g = 4 * b + q
                        for r in range(2):
                            ins = nc.tensor.matmul(bank(i0 + b)[0:NCH, q * P:(q + 1) * P], hin[:, r, 16 * hf + g, :],
                                                   w[:, r, g, :], start=(r == 0), stop=(r == 1))
                    ins.then_inc(full[(i0 + b) % 8], 1)
            @block.vector
            def _(dve):
                for b in range(8):
                    dve.wait_ge(*emptied(i0 - 1 - b))
            add_y(i0, 4, 16 * hf)
        y_ready = [emptied(i0 - 4 + b) for b in range(8)]

        g_s = view("H", 0, 4096, NCH).rearrange("p (s c) -> p s c", s=S)

        @block.scalar
        def _(act):
            for m in y_ready:
                act.wait_ge(*m)
            for s in range(S):
                ins = nc.scalar.activation(g_s[:, s].rearrange("p (g c) -> p g c", g=G), u_c[:, :, s, :], ACT.Gelu_apprx_tanh)
            ins.then_inc(*act_did.up())
        g_ready = act_did.now()

        gT = view("D", 0, 2560).rearrange("p (k n s) -> p k n s", k=4, s=S)
        oaT = view("D", 2560, 2560).rearrange("p (k t) -> p k t", k=4)
        gT_ready = transposes([[g_s[:, s, b * P:(b + 1) * P] for b in range(4)] for s in range(S)],
                              lambda s: gT[:, :, :, s], [g_ready])
        slot, w, w_mark = load_weights(I["s5_w_glu"][0].rearrange("(k p) n -> p k n", p=P),
                                       lambda a: a[:, 0:2048].rearrange("p (k n) -> p k n", k=4))
        i0 = take(8)
        w_last[slot] = [filled(i0 + 7)]
        gT_flat = view("D", 0, 2560).rearrange("p (k t) -> p k t", k=4)
        halves = [(0, 512), (512, 128)]

        @block.tensor
        def _(pe):
            for m in gT_ready:
                pe.wait_ge(*m)
            pe.wait_ge(*w_mark)
            for b in range(4):
                for n, (t0, tn) in enumerate(halves):
                    i = i0 + 2 * b + n
                    open_bank(pe, i)
                    for k in range(4):
                        ins = nc.tensor.matmul(bank(i)[:, 0:tn], w[:, k, b * P:(b + 1) * P], gT_flat[:, k, t0:t0 + tn],
                                               start=(k == 0), stop=(k == 3))
                    ins.then_inc(full[i % 8], 1)

        @block.scalar
        def _(act):
            for b in range(4):
                for n, (t0, tn) in enumerate(halves):
                    i = i0 + 2 * b + n
                    act.wait_ge(*filled(i))
                    nc.scalar.activation(oaT[:, b, t0:t0 + tn], bank(i)[:, 0:tn], ACT.Sigmoid).then_inc(free[i % 8], 1)
        glu_ready = [emptied(i0 + n) for n in range(8)]

        @block.vector
        def _(dve):
            for m in glu_ready:
                dve.wait_ge(*m)
            link(dve, dve_did, nc.vector.tensor_tensor(oaT, oaT, gT_flat, ALU.mult))
        oa_ready = dve_did.now()

        zq = view("C", 0, 7680).rearrange("p (t n) -> p t n", t=NT)
        gain = view("MOD", 6144, 1024)
        vctx = view("E", 1024, 512)
        kctx = view("E", 1536, 512)
        sub_row = view("E", 512, 128)

        ld = group("loads_in")
        @block.sync
        def _(sp):
            sp.wait_ge(*oa_ready)
            for n, src in enumerate((I["diff_q_norm"], I["diff_k_norm"])):
                sp.dma_start(gain[:, 512 * n:512 * n + 512].rearrange("p (g d) -> p g d", d=DK),
                             src.unsqueeze(1).to_broadcast([P, 8, DK])).then_inc(*ld.up())
            sp.dma_start(kctx, I["cache_diff_k"].rearrange("b e t m h d -> (b e t) (m h d)")).then_inc(*ld.up())
            sp.dma_start(vctx, I["cache_diff_v"].rearrange("b e t h d -> (b e t) (h d)")).then_inc(*ld.up())
            sp.dma_start(sub_row, I["diff_sub_norm"].to_broadcast([P, P])).then_inc(*ld.up())
        ctx_in = ld.now()
        z_ready = []
        for n in range(3):
            z_ready = project(I["even_w_in"][0], 512 + 512 * n, 512, lambda t, n=n: zq[:, t, 512 * n:512 * n + 512],
                              hT_ready + y_ready + [g_ready] + gT_ready)
        qk_ready = qk_norm_rope(lambda t: zq[:, t, :], 1024, gain, view("D", 0, 1024), z_ready + [ctx_in, oa_ready])

        st = group("stores_out")
        @block.sync
        def _(sp):
            sp.wait_ge(*qk_ready[0])
            sp.dma_start(O["new_diff_k"].rearrange("b e t m h d -> (b e t) (m h d)"), zq[:, 0, 512:1024]).then_inc(*st.up())
            sp.dma_start(O["new_diff_v"].rearrange("b e t h d -> (b e t) (h d)"), zq[:, 0, 1024:1536]).then_inc(*st.up())
        qT = view("C", 7680, 2560).rearrange("p (b t) -> p b t", b=4)
        kT = view("MISC", 0, 2560).rearrange("p (b t) -> p b t", b=4)
        kcT = view("MISC", 2560, 512).rearrange("p (b t) -> p b t", b=4)
        qT_ready = transposes([[zq[:, t, b * P:(b + 1) * P] for b in range(4)] for t in range(NT)],
                              lambda t: qT[:, :, t * P:(t + 1) * P], qk_ready)
        kT_ready = transposes([[zq[:, t, 512 + b * P:512 + (b + 1) * P] for b in range(4)] for t in range(NT)],
                              lambda t: kT[:, :, t * P:(t + 1) * P], qk_ready)
        kc_ready = transposes([[kctx[:, b * P:(b + 1) * P] for b in range(4)]], lambda n: kcT, [ctx_in])
        prob = view("D", 0, 1280).rearrange("p (m k) -> p m k", m=2)
        aT = view("D", 1280, 640).rearrange("p (b q) -> p b q", b=5)
        ob = view("D", 1920, 512)
        obT = view("HT", 0, 2560).rearrange("p (k t) -> p k t", k=4)
        pe_attn = qT_ready + kT_ready + kc_ready
        for t in range(NT):
            nkb = 1 if t == 0 else 5
            for hd in range(4):
                parts = [(0, P, None)] if t == 0 else [(0, P, "ctx"), (P, 512, "own")]
                i0 = take(2 * len(parts))

                @block.tensor
                def _(pe):
                    for m in pe_attn:
                        pe.wait_ge(*m)
                    for m in range(2):
                        g = 4 * m + hd
                        rows = slice(64 * (g % 2), 64 * (g % 2) + 64)
                        for n, (k0, kn, what) in enumerate(parts):
                            i = i0 + m * len(parts) + n
                            open_bank(pe, i)
                            keys = {None: kT[rows, g // 2, 0:P], "ctx": kcT[rows, g // 2, :], "own": kT[rows, g // 2, P:TOK]}[what]
                            nc.tensor.matmul(bank(i)[:, 0:kn], qT[rows, g // 2, t * P:(t + 1) * P], keys,
                                             start=True, stop=True).then_inc(full[i % 8], 1)
                pe_attn = []
                np_ = len(parts)

                @block.vector
                def _(dve):
                    for m in range(2):
                        for n, (k0, kn, what) in enumerate(parts):
                            i = i0 + m * np_ + n
                            dve.wait_ge(*filled(i))
                            nc.vector.tensor_reduce(stat[:, 2 * m + n:2 * m + n + 1], bank(i)[:, 0:kn], AX, ALU.max).then_inc(*dve_did.up())
                    dve.wait_ge(*dve_did.now())
                    mx = stat[:, 0:4].rearrange("p (m n) -> p m n", n=2)
                    if np_ == 2:
                        link(dve, dve_did, nc.vector.tensor_tensor(mx[:, :, 0], mx[:, :, 0], mx[:, :, 1], ALU.max))
                    link(dve, dve_did, nc.vector.tensor_scalar(stat[:, 4:6], mx[:, :, 0], -SCALE, None, ALU.mult))
                max_ready = dve_did.now()

                @block.scalar
                def _(act):
                    act.wait_ge(*max_ready)
                    for m in range(2):
                        for n, (k0, kn, what) in enumerate(parts):
                            i = i0 + m * np_ + n
                            nc.scalar.activation(prob[:, m, k0:k0 + kn], bank(i)[:, 0:kn], ACT.Exp, bias=stat[:, 4 + m:5 + m],
                                                 scale=SCALE, accum_out=stat[:, 8 + 2 * m + n:9 + 2 * m + n]).then_inc(free[i % 8], 1)
                exp_ready = [emptied(i0 + n) for n in range(2 * np_)]

                @block.vector
                def _(dve):
                    for m in exp_ready:
                        dve.wait_ge(*m)
                    z4 = stat[:, 8:12].rearrange("p (m n) -> p m n", n=2)
                    if np_ == 2:
                        link(dve, dve_did, nc.vector.tensor_tensor(stat[:, 6:8], z4[:, :, 0], z4[:, :, 1], ALU.add))
                    else:
                        link(dve, dve_did, nc.vector.tensor_copy(stat[:, 6:8], z4[:, :, 0]))
                    link(dve, dve_did, nc.vector.reciprocal(stat[:, 12:14], stat[:, 6:8]))
                    link(dve, dve_did, nc.vector.tensor_tensor(stat[:, 13:14], stat[:, 13:14], lam_col, ALU.mult))
                    w_ = nkb * P
                    link(dve, dve_did, nc.vector.tensor_scalar(prob[:, 1, 0:w_], prob[:, 1, 0:w_], stat[:, 13:14], None, ALU.mult))
                    link(dve, dve_did, nc.vector.scalar_tensor_tensor(prob[:, 0, 0:w_], prob[:, 0, 0:w_], stat[:, 12:13], prob[:, 1, 0:w_], ALU.mult, ALU.subtract))
                blocks = [prob[:, 0, b * P:(b + 1) * P] for b in range(nkb)]
                groups = [blocks[0:4]] + ([blocks[4:5]] if nkb > 4 else [])
                aT_ready = transposes(groups, lambda n, nkb=nkb: aT[:, 4 * n:min(4 * n + 4, nkb), :], [dve_did.now()])
                i1 = take(1)

                @block.tensor
                def _(pe):
                    for m in aT_ready:
                        pe.wait_ge(*m)
                    open_bank(pe, i1)
                    vals = [zq[:, 0, 1024 + hd * P:1024 + (hd + 1) * P]] if t == 0 else \
                        [vctx[:, hd * P:(hd + 1) * P]] + [zq[:, b, 1024 + hd * P:1024 + (hd + 1) * P] for b in range(1, NT)]
                    for b in range(nkb):
                        ins = nc.tensor.matmul(bank(i1)[:, 0:P], aT[:, b, :], vals[b], start=(b == 0), stop=(b == nkb - 1))
                    ins.then_inc(full[i1 % 8], 1)

                @block.scalar
                def _(act):
                    act.wait_ge(*filled(i1))
                    nc.scalar.copy(ob[:, hd * P:(hd + 1) * P], bank(i1)[:, 0:P]).then_inc(free[i1 % 8], 1)
            ob_marks = [emptied(i1 - b) for b in range(8)]
            sqv = view("E", 0, 512)

            @block.vector
            def _(dve):
                for m in ob_marks:
                    dve.wait_ge(*m)
                o3 = ob.rearrange("p (h d) -> p h d", h=4)
                s3 = sqv.rearrange("p (h d) -> p h d", h=4)
                link(dve, dve_did, nc.vector.tensor_tensor(sqv, ob, ob, ALU.mult))
                link(dve, dve_did, nc.vector.tensor_reduce(stat[:, 0:4], s3, AX, ALU.add))
                link(dve, dve_did, nc.vector.tensor_scalar(stat[:, 0:4], stat[:, 0:4], 1.0 / P, EPS, ALU.mult, ALU.add))
            var_ready = dve_did.now()

            @block.scalar
            def _(act):
                act.wait_ge(*var_ready)
                nc.scalar.activation(stat[:, 16:20], stat[:, 0:4], ACT.Sqrt).then_inc(*act_did.up())
            std_ready = act_did.now()

            @block.vector
            def _(dve):
                dve.wait_ge(*std_ready)
                o3 = ob.rearrange("p (h d) -> p h d", h=4)
                link(dve, dve_did, nc.vector.reciprocal(stat[:, 20:24], stat[:, 16:20]))
                link(dve, dve_did, nc.vector.tensor_scalar(stat[:, 20:24], stat[:, 20:24], 1.0 - LAM_INIT, None, ALU.mult))
                link(dve, dve_did, nc.vector.tensor_tensor(o3, o3, stat[:, 20:24].unsqueeze(2).to_broadcast([P, 4, P]), ALU.mult))
                link(dve, dve_did, nc.vector.tensor_tensor(o3, o3, sub_row.unsqueeze(1).to_broadcast([P, 4, P]), ALU.mult))
            ob_done = transposes([[ob[:, b * P:(b + 1) * P] for b in range(4)]], lambda n, t=t: obT[:, :, t * P:(t + 1) * P], [dve_did.now()])

            @block.vector
            def _(dve):
                dve.wait_ge(*ob_done[0])

            @block.scalar
            def _(act):
                act.wait_ge(*ob_done[0])
        out_project(I["even_w_out"][0], lambda k: oaT[:, k, :] if k < 4 else obT[:, k - 4, :], ob_done + [oa_ready])

        slot_in = [sem(f"expert_row_in{j}") for j in range(RING)]
        u_used, v_used, diag_ready = sem("u_rows_used"), sem("v_rows_used"), sem("diagonals_ready")
        staged, w_staged, granted = sem("indices_staged"), sem("weights_staged"), sem("slots_granted")
        ring = arena[:, at["HT"]:at["HT"] + RING * D].rearrange("p (j d) -> p j d", j=RING)
        s_all = view("C", 0, 10240).rearrange("p (t n) -> p t n", t=NT)
        sub_k = view("MOD", 0, 2048).rearrange("p (c k) -> p c k", c=16)
        qpT = view("MISC", 0, 2560).rearrange("p (c t) -> p c t", c=4)

        def dview(start, size):
            o = at["D"] + start
            return arena[:, o:o + size]
        vals1 = dview(0, 256).rearrange("p (c k) -> p c k", c=16)
        idx1 = dview(256, 256).bitcast(U32).rearrange("p (c k) -> p c k", c=16)
        idx1f = dview(512, 256).rearrange("p (c k) -> p c k", c=16)
        cand = dview(768, 256)
        best = dview(1024, 128).rearrange("p (h k) -> p h k", h=HEADS)
        pos = dview(1152, 128).bitcast(U32)
        j1f, j2f = dview(1280, 128), dview(1408, 128)
        e1f, e2f = dview(1536, 128), dview(1664, 128)
        sel = dview(1792, 2048)
        expert = dview(3840, 640).bitcast(U32).rearrange("p (t n) -> p t n", t=NT)
        gate = dview(4480, 640).rearrange("p (t n) -> p t n", t=NT)
        act_all = dview(5120, 640).rearrange("p (t n) -> p t n", t=NT)
        w_all = dview(5760, 128)
        diag = dview(5888, 512).rearrange("p (s n) -> p s n", s=4)
        posj = dview(6400, 128).bitcast(U32)
        islot = dview(6528, 32).bitcast(U32).rearrange("p (s n) -> p s n", s=2)
        aslot = dview(6560, 32)
        wslot = dview(6592, 32).rearrange("p (s n) -> p s n", s=2)
        esum = dview(6624, 16)
        zero_mv = dview(6656, 256).bitcast(BF16)
        peer_rounds = [0]
        peer_tiles = [0]
        stages = [0]

        @block.tensor
        def _(pe):
            pe.sem_inc(v_used, DIAGS)

        def route_scores(l, ready):
            ld = group("loads_in")
            @block.sync
            def _(sp):
                sp.wait_ge(*dve_did.now())
                sp.dma_start(sub_k, I["peer_sub_keys"][l]).then_inc(*ld.up())
            keys_in = ld.now()
            for blk in range(4):
                slot, w, w_mark = load_weights(I["peer_w_q"][l].rearrange("(k p) n -> p k n", p=P)[:, :, blk * 512:(blk + 1) * 512],
                                               lambda a: a.rearrange("p (k n) -> p k n", k=KD))
                i0 = take(8)
                w_last[slot] = [filled(i0 + 7)]
                i1 = take(NT)

                @block.tensor
                def _(pe):
                    if blk == 0:
                        for m in ready:
                            pe.wait_ge(*m)
                        pe.wait_ge(*keys_in)
                    pe.wait_ge(*w_mark)
                    for c in range(4):
                        for n, (t0, tn) in enumerate(halves):
                            i = i0 + 2 * c + n
                            open_bank(pe, i)
                            for k in range(KD):
                                ins = nc.tensor.matmul(bank(i)[:, 0:tn], w[:, k, c * P:(c + 1) * P], hT[:, k, t0:t0 + tn],
                                                       start=(k == 0), stop=(k == KD - 1))
                            ins.then_inc(full[i % 8], 1)
                    for n in range(8):
                        pe.wait_ge(*emptied(i0 + n))
                    for t in range(NT):
                        open_bank(pe, i1 + t)
                        for c in range(4):
                            ins = nc.tensor.matmul(bank(i1 + t)[:, c * P:(c + 1) * P], qpT[:, c, t * P:(t + 1) * P], sub_k[:, 4 * blk + c, :],
                                                   start=True, stop=True)
                        ins.then_inc(full[(i1 + t) % 8], 1)

                @block.scalar
                def _(act):
                    for c in range(4):
                        for n, (t0, tn) in enumerate(halves):
                            i = i0 + 2 * c + n
                            act.wait_ge(*filled(i))
                            nc.scalar.copy(qpT[:, c, t0:t0 + tn], bank(i)[:, 0:tn]).then_inc(free[i % 8], 1)
                    for t in range(NT):
                        act.wait_ge(*filled(i1 + t))
                        nc.scalar.copy(s_all[:, t, blk * 512:(blk + 1) * 512], bank(i1 + t)).then_inc(free[(i1 + t) % 8], 1)

        def top16(dve, v, src, out, idx):
            link(dve, dve_did, v.max(out[:, 0:8], src))
            link(dve, dve_did, v.max_index(idx[:, 0:8], out[:, 0:8], src))
            link(dve, dve_did, v.match_replace(src, out[:, 0:8], src, -3.0e38))
            link(dve, dve_did, v.max(out[:, 8:16], src))
            link(dve, dve_did, v.max_index(idx[:, 8:16], out[:, 8:16], src))

        def route(l, t):
            @block.vector
            def _(dve):
                v = nc.vector
                for c in range(16):
                    top16(dve, v, s_all[:, t, c * P:(c + 1) * P], vals1[:, c], idx1[:, c])
                link(dve, dve_did, v.tensor_copy(idx1f, idx1))
                pos3 = pos.rearrange("p (h k) -> p h k", h=HEADS)
                for hd in range(HEADS):
                    link(dve, dve_did, v.tensor_tensor(
                        cand.rearrange("p (a b) -> p a b", a=TOPK), vals1[:, 2 * hd].unsqueeze(2).to_broadcast([P, TOPK, TOPK]),
                        vals1[:, 2 * hd + 1].unsqueeze(1).to_broadcast([P, TOPK, TOPK]), ALU.add))
                    top16(dve, v, cand, best[:, hd], pos3[:, hd])
                link(dve, dve_did, v.tensor_scalar(posj, pos, 4, None, ALU.logical_shift_right))
                link(dve, dve_did, v.tensor_copy(j1f, posj))
                link(dve, dve_did, v.tensor_scalar(posj, pos, 15, None, ALU.bitwise_and))
                link(dve, dve_did, v.tensor_copy(j2f, posj))
                sel3 = sel.rearrange("p (n j) -> p n j", j=TOPK)
                sel4 = sel.rearrange("p (h k j) -> p h k j", h=HEADS, k=TOPK)
                idx4 = idx1f.rearrange("p (h c) k -> p h c k", c=2)
                for half, (jf, ef) in enumerate(((j1f, e1f), (j2f, e2f))):
                    link(dve, dve_did, v.tensor_tensor(sel3, jf.unsqueeze(2).to_broadcast([P, HK, TOPK]),
                                                       iota16.unsqueeze(1).to_broadcast([P, HK, TOPK]), ALU.is_equal))
                    link(dve, dve_did, v.tensor_tensor(sel4, sel4, idx4[:, :, half].unsqueeze(2).to_broadcast([P, HEADS, TOPK, TOPK]), ALU.mult))
                    link(dve, dve_did, v.tensor_reduce(ef, sel3, AX, ALU.add))
                link(dve, dve_did, v.tensor_scalar(e1f, e1f, 128.0, float(l * EXPERTS), ALU.mult, ALU.add))
                link(dve, dve_did, v.tensor_tensor(e1f, e1f, e2f, ALU.add))
                link(dve, dve_did, v.tensor_copy(expert[:, t], e1f))
                g3 = gate[:, t].rearrange("p (h k) -> p h k", h=HEADS)
                link(dve, dve_did, v.tensor_tensor(g3, best, best[:, :, 0:1].to_broadcast([P, HEADS, TOPK]), ALU.subtract))
            shifted = dve_did.now()

            @block.scalar
            def _(act):
                act.wait_ge(*shifted)
                nc.scalar.activation(gate[:, t], gate[:, t], ACT.Exp).then_inc(*act_did.up())
            exped = act_did.now()

            @block.vector
            def _(dve):
                v = nc.vector
                dve.wait_ge(*exped)
                g3 = gate[:, t].rearrange("p (h k) -> p h k", h=HEADS)
                link(dve, dve_did, v.tensor_reduce(esum[:, 0:8], g3, AX, ALU.add))
                link(dve, dve_did, v.reciprocal(esum[:, 8:16], esum[:, 0:8]))
                link(dve, dve_did, v.tensor_tensor(g3, g3, esum[:, 8:16].unsqueeze(2).to_broadcast([P, HEADS, TOPK]), ALU.mult))
            return dve_did.now()

        def gather_rounds(table, t, round0, free_first, free_sem, free_base, routed):
            s0 = peer_rounds[0]
            peer_rounds[0] += ROUNDS

            def one_round(pool, r, parity, wait_of):
                nc.gpsimd.tensor_copy(islot[:, parity], expert[:, t, bass.ds(r * RING, RING)]).then_inc(staged, 1)
                for j in range(RING):
                    if j == 0:
                        pool.wait_ge(staged, r + (s0 + 1))
                        pool.sem_inc(granted, 1)
                    wait_of(j)
                    pool.sem_inc(granted, 1)
                    nc.gpsimd.indirect_dma_start(out=ring[:, j, :], out_offset=None, in_=table,
                                                 in_offset=bass.IndirectOffsetOnAxis(ap=islot[:, parity, j:j + 1], axis=0)
                                                 ).then_inc(slot_in[j], 16)

            @block.gpsimd
            def _(pool):
                pool.wait_ge(*routed)
                for r in range(2):
                    def first_wait(j, r=r):
                        if r:
                            pool.wait_ge(free_sem, free_base + j + 1)
                        elif free_first is not None:
                            pool.wait_ge(free_first[0], free_first[1] + j + 1)
                    one_round(pool, r, r, first_wait)
                with pool.Fori(1, ROUNDS // 2) as i:
                    for parity in range(2):
                        def wait(j, parity=parity):
                            pool.wait_ge(free_sem, (i * 2 + parity - 1) * RING + (free_base + j + 1))
                        one_round(pool, i * 2 + parity, parity, wait)
            return s0

        def peer_tile(l, k, t, routed, tables):
            s_u = gather_rounds(tables[0], t, 0, (v_used, DIAGS + HK * k - RING) if k else None, u_used, HK * k, routed)
            s_v = gather_rounds(tables[1], t, 0, (u_used, HK * (k + 1) - RING), v_used, DIAGS + HK * k, routed)

            @block.vector
            def _(dve):
                with dve.Fori(0, ROUNDS // 2) as i:
                    for parity in range(2):
                        for j in range(RING):
                            dve.wait_ge(slot_in[j], i * 32 + (16 * (s_u + parity) + 16))
                            nc.vector.tensor_tensor_reduce(ring[:, j, :], ring[:, j, :], h[:, t, :], 1.0, 0.0, ALU.mult, ALU.add,
                                                           aslot[:, 16 * parity + j:16 * parity + j + 1]).then_inc(u_used, 1)
                    dve.wait_ge(u_used, i * 32 + (HK * k + 32))
                    dve.wait_ge(*routed)
                    nc.vector.tensor_copy(act_all[:, t, bass.ds(i * 32, 32)], aslot).then_inc(dots_kept.sem, 1)
                    dve.wait_ge(dots_kept.sem, i + (dots_kept.n + 1))
            dots_kept.n += ROUNDS // 2
            dots = dots_kept.now()

            @block.scalar
            def _(act):
                act.wait_ge(*dots)
                nc.scalar.activation(act_all[:, t], act_all[:, t], ACT.Gelu_apprx_tanh).then_inc(*act_did.up())
            gelued = act_did.now()

            @block.vector
            def _(dve):
                dve.wait_ge(*gelued)
                if k:
                    dve.wait_ge(w_staged, ROUNDS * k)
                nc.vector.tensor_tensor(w_all, act_all[:, t], gate[:, t], ALU.mult).then_inc(*dve_did.up())
            weighted = dve_did.now()

            @block.scalar
            def _(act):
                act.wait_ge(*weighted)
                with act.Fori(0, ROUNDS // 2) as i:
                    for parity in range(2):
                        nc.scalar.copy(wslot[:, parity], w_all[:, bass.ds((i * 2 + parity) * RING, RING)]).then_inc(w_staged, 1)
                        act.wait_ge(w_staged, i * 2 + (ROUNDS * k + parity + 1))
                        for j in range(RING):
                            act.wait_ge(v_used, i * 32 + (HK * k + parity * RING + j + 1))
                            nc.scalar.activation(diag[:, j % DIAGS], ident, ACT.Copy, scale=wslot[:, parity, j:j + 1]).then_inc(diag_ready, 1)
            i0 = take(2)

            @block.tensor
            def _(pe):
                for n in range(2):
                    open_bank(pe, i0 + n)
                    nc.tensor.matmul(bank(i0 + n), zero_w, zero_mv, start=True, stop=False)
                with pe.Fori(0, ROUNDS // 2) as i:
                    for parity in range(2):
                        for j in range(RING):
                            pe.wait_ge(slot_in[j], i * 32 + (16 * (s_v + parity) + 16))
                            pe.wait_ge(diag_ready, i * 32 + (HK * k + parity * RING + j + 1))
                            nc.tensor.matmul(bank(i0), diag[:, j % DIAGS], ring[:, j, 0:512], start=False, stop=False)
                            nc.tensor.matmul(bank(i0 + 1), diag[:, j % DIAGS], ring[:, j, 512:1024], start=False, stop=False).then_inc(v_used, 1)
                for n in range(2):
                    nc.tensor.matmul(bank(i0 + n), zero_w, zero_mv, start=False, stop=True).then_inc(full[(i0 + n) % 8], 1)
            return i0

        dots_kept = count("dots_kept")

        def peer(l):
            ready = modulate(l, 1, I["norm_ffn"])
            route_scores(l, ready)

            @block.vector
            def _(dve):
                dve.wait_ge(*emptied(state["items"] - 1))
                link(dve, dve_did, nc.vector.memset(zero_mv, 0.0))
            meet()
            tables = [I["peer_u"].rearrange("l e d -> (l e) d"), I["peer_v"].rearrange("l e d -> (l e) d")]
            routed = route(l, 0)
            for t in range(NT):
                k = peer_tiles[0]
                peer_tiles[0] += 1
                i0 = peer_tile(l, k, t, routed, tables)
                if t + 1 < NT:
                    routed = route(l, t + 1)

                @block.vector
                def _(dve):
                    for n in range(2):
                        dve.wait_ge(*filled(i0 + n))
                        add_gated(dve, t, n, bank(i0 + n), free[(i0 + n) % 8], sel[:, 0:512])
            meet()

        peer(0)

        hT_ready = modulate(1, 0, I["norm_mix"])
        zo = view("C", 0, NT * ODD_IN).rearrange("p (t n) -> p t n", t=NT)
        pool_m = view("MISC", 0, 3072).rearrange("p (m w s) -> p m w s", m=6, w=4)
        gain1 = view("MOD", 6144, 640)
        pw_sb = view("E", 1536, 512).rearrange("p (w d) -> p w d", w=4)
        kc1 = view("E", 1024, 128)
        vc1 = view("E", 1152, 128)

        ld = group("loads_in")
        @block.sync
        def _(sp):
            sp.wait_ge(*hT_ready[-1])
            sp.wait_ge(*dve_did.now())
            sp.dma_start(pool_m.rearrange("p m w s -> p (m w s)"), I["pool_bands"]).then_inc(*ld.up())
            sp.dma_start(gain1[:, 0:512].rearrange("p (g d) -> p g d", d=DK), I["win_q_norm"].unsqueeze(1).to_broadcast([P, 8, DK])).then_inc(*ld.up())
            sp.dma_start(gain1[:, 512:640].rearrange("p (g d) -> p g d", d=DK), I["win_k_norm"].unsqueeze(1).to_broadcast([P, 2, DK])).then_inc(*ld.up())
            sp.dma_start(kc1, I["cache_win_k"].rearrange("b e t h d -> (b e t) (h d)")).then_inc(*ld.up())
            sp.dma_start(vc1, I["cache_win_v"].rearrange("b e t h d -> (b e t) (h d)")).then_inc(*ld.up())
            sp.dma_start(sink_col, I["win_sink"].to_broadcast([P, 8])).then_inc(*ld.up())
            sp.dma_start(pw_sb, I["pool_w"][0].rearrange("w c d -> c w d")).then_inc(*ld.up())
            with nc.allow_non_contiguous_dma(reason="a short column vector"):
                sp.dma_start(pscale_col, I["pool_scale"].rearrange("a (w d) -> d (a w)", w=4)).then_inc(*ld.up())
        ctx_in = ld.now()
        for col0, n in ((0, 512), (512, 256), (768, 512)):
            z_ready = project(I["odd_w_in"][0], col0, n, lambda t, col0=col0, n=n: zo[:, t, col0:col0 + n], hT_ready)
        z_ready = [emptied(state["items"] - 1 - b) for b in range(8)]
        qk_ready = qk_norm_rope(lambda t: zo[:, t, :], 640, gain1, view("D", 0, 1024), z_ready + [ctx_in])

        st = group("stores_out")
        @block.sync
        def _(sp):
            sp.wait_ge(*qk_ready[0])
            sp.dma_start(O["new_win_k"].rearrange("b e t h d -> (b e t) (h d)"), zo[:, 0, 512:640]).then_inc(*st.up())
            sp.dma_start(O["new_win_v"].rearrange("b e t h d -> (b e t) (h d)"), zo[:, 0, 640:768]).then_inc(*st.up())

        kdup = view("D", 0, 6 * 256).rearrange("p (t n r d) -> p t n r d", t=6, n=2, r=2)

        @block.vector
        def _(dve):
            for r in range(2):
                for t in range(NT):
                    nc.vector.tensor_copy(kdup[:, t, :, r, :], zo[:, t, 512:640].rearrange("p (n d) -> p n d", n=2)).then_inc(*dve_did.up())
                nc.vector.tensor_copy(kdup[:, 5, :, r, :], kc1.rearrange("p (n d) -> p n d", n=2)).then_inc(*dve_did.up())
        dup_ready = dve_did.now()
        qT1 = view("C", 6400, 2560).rearrange("p (b t) -> p b t", b=4)
        qT_ready = transposes([[zo[:, t, b * P:(b + 1) * P] for b in range(4)] for t in range(NT)],
                              lambda t: qT1[:, :, t * P:(t + 1) * P], qk_ready)
        kT1 = view("D", 1536, 1536).rearrange("p (n t) -> p n t", n=2)
        kT_ready = transposes([[kdup[:, t, n].rearrange("p r d -> p (r d)") for n in range(2)] for t in range(6)],
                              lambda t: kT1[:, :, t * P:(t + 1) * P], [dup_ready])
        oc = view("D", 3072, 512)
        prob1 = view("D", 3584, 512)
        aT1 = view("D", 4096, 512).rearrange("p (b q) -> p b q", b=4)
        ocT = view("HT", 0, 2560).rearrange("p (k t) -> p k t", k=4)
        odT = view("HT", 2560, 2560).rearrange("p (k t) -> p k t", k=4)
        plT = view("E", 0, 640)
        z_all_read = z_ready
        for wd in range(4):
            i0 = take(2)

            @block.tensor
            def _(pe):
                if wd == 0:
                    for m in z_ready + [ctx_in]:
                        pe.wait_ge(*m)
                for t in range(NT):
                    i = i0 + (0 if t < 4 else 1)
                    if t in (0, 4):
                        open_bank(pe, i)
                    o = bank(i)[:, (t % 4) * P:(t % 4) * P + P]
                    srcs = [(t, 0 if t == 0 else 1 if t == 1 else 3 if t == 4 else 2)]
                    if t > 1:
                        srcs.append((t - 1, 4))
                    if 0 < t < 4:
                        srcs.append((t + 1, 5))
                    for n, (tt, m) in enumerate(srcs):
                        ins = nc.tensor.matmul(o, zo[:, tt, 768 + wd * P:768 + (wd + 1) * P], pool_m[:, m, wd, :],
                                               start=(n == 0), stop=(n == len(srcs) - 1))
                    if t >= 3:
                        ins.then_inc(full[i % 8], 1)
            before = [emptied(i0 - 1), emptied(i0 - 2)]

            @block.scalar
            def _(act):
                for m in before:
                    act.wait_ge(*m)
                act.wait_ge(*filled(i0))
                nc.scalar.copy(plT[:, 0:512], bank(i0)).then_inc(free[i0 % 8], 1)
                act.wait_ge(*filled(i0 + 1))
                nc.scalar.copy(plT[:, 512:640], bank(i0 + 1)[:, 0:P]).then_inc(free[(i0 + 1) % 8], 1)
            i1 = take(2)

            @block.tensor
            def _(pe):
                for n, (t0, tn) in enumerate(halves):
                    open_bank(pe, i1 + n)
                    pe.wait_ge(*emptied(i0 + n))
                    nc.tensor.matmul(bank(i1 + n)[:, 0:tn], pw_sb[:, wd, :], plT[:, t0:t0 + tn], start=True, stop=True).then_inc(full[(i1 + n) % 8], 1)

            @block.scalar
            def _(act):
                for n, (t0, tn) in enumerate(halves):
                    act.wait_ge(*filled(i1 + n))
                    nc.scalar.activation(odT[:, wd, t0:t0 + tn], bank(i1 + n)[:, 0:tn], ACT.Copy, scale=pscale_col[:, wd:wd + 1]).then_inc(free[(i1 + n) % 8], 1)
        od_ready = [emptied(state["items"] - 1 - b) for b in range(8)]

        for t in range(NT):
            if t == 0:
                segs, nkb, masks = [(0, 0, P)], 1, []
                vals = [zo[:, 0, 640:768]]
            else:
                lo, hi = max(t - 1, 1), min(t + 1, 4)
                nkb = 1 + hi - lo + 1
                segs = [(0, 5 * P, P), (P, lo * P, (hi - lo + 1) * P)]
                masks = ([(P, mask_before)] if t > 1 else []) + ([((nkb - 1) * P, mask_after)] if t < 4 else [])
                vals = [vc1] + [zo[:, b, 640:768] for b in range(lo, hi + 1)]
            width = nkb * P
            for hd in range(8):
                kv, rows = hd // 4, slice(64 * (hd % 2), 64 * (hd % 2) + 64)
                i0 = take(1)

                @block.tensor
                def _(pe):
                    if t == 0 and hd == 0:
                        for m in qT_ready + kT_ready:
                            pe.wait_ge(*m)
                    open_bank(pe, i0)
                    for (o, k0, kn) in segs:
                        ins = nc.tensor.matmul(bank(i0)[:, o:o + kn], qT1[rows, hd // 2, t * P:(t + 1) * P], kT1[rows, kv, k0:k0 + kn],
                                               start=True, stop=True)
                    ins.then_inc(full[i0 % 8], 1)

                @block.vector
                def _(dve):
                    dve.wait_ge(*filled(i0))
                    for o, mask in masks:
                        link(dve, dve_did, nc.vector.tensor_tensor(bank(i0)[:, o:o + P], bank(i0)[:, o:o + P], mask, ALU.add))
                    link(dve, dve_did, nc.vector.tensor_reduce(stat[:, 0:1], bank(i0)[:, 0:width], AX, ALU.max))
                    link(dve, dve_did, nc.vector.tensor_scalar(stat[:, 1:2], stat[:, 0:1], SCALE, sink_col[:, hd:hd + 1], ALU.mult, ALU.max))
                    link(dve, dve_did, nc.vector.tensor_scalar(stat[:, 2:3], stat[:, 1:2], -1.0, None, ALU.mult))
                max_ready = dve_did.now()

                @block.scalar
                def _(act):
                    act.wait_ge(*max_ready)
                    nc.scalar.activation(stat[:, 4:5], sink_col[:, hd:hd + 1], ACT.Exp, bias=stat[:, 2:3])
                    nc.scalar.activation(prob1[:, 0:width], bank(i0)[:, 0:width], ACT.Exp, bias=stat[:, 2:3], scale=SCALE,
                                         accum_out=stat[:, 3:4]).then_inc(free[i0 % 8], 1)
                p_ready = emptied(i0)
                aT_ready = transposes([[prob1[:, b * P:(b + 1) * P] for b in range(nkb)]], lambda n, nkb=nkb: aT1[:, 0:nkb, :], [p_ready])
                i1 = take(1)

                @block.vector
                def _(dve):
                    dve.wait_ge(*p_ready)
                    link(dve, dve_did, nc.vector.tensor_tensor(stat[:, 5:6], stat[:, 3:4], stat[:, 4:5], ALU.add))
                    link(dve, dve_did, nc.vector.reciprocal(stat[:, 6:7], stat[:, 5:6]))

                @block.tensor
                def _(pe):
                    for m in aT_ready:
                        pe.wait_ge(*m)
                    open_bank(pe, i1)
                    for b in range(nkb):
                        ins = nc.tensor.matmul(bank(i1)[:, 0:DK], aT1[:, b, :], vals[b][:, kv * DK:(kv + 1) * DK], start=(b == 0), stop=(b == nkb - 1))
                    ins.then_inc(full[i1 % 8], 1)

                @block.vector
                def _(dve):
                    dve.wait_ge(*filled(i1))
                    nc.vector.tensor_scalar(oc[:, hd * DK:(hd + 1) * DK], bank(i1)[:, 0:DK], stat[:, 6:7], None, ALU.mult).then_inc(free[i1 % 8], 1)
            oc_marks = [emptied(i1 - b) for b in range(8)]
            oc_done = transposes([[oc[:, b * P:(b + 1) * P] for b in range(4)]], lambda n, t=t: ocT[:, :, t * P:(t + 1) * P], oc_marks)

            @block.vector
            def _(dve):
                dve.wait_ge(*oc_done[0])
        out_project(I["odd_w_out"][0], lambda k: ocT[:, k, :] if k < 4 else odT[:, k - 4, :], od_ready + oc_done)
        peer(1)

        st = group("stores_out")
        @block.sync
        def _(sp):
            sp.dma_start(O["y_prompt"][0], x[:, 0, :]).then_inc(*st.up())
            sp.dma_start(O["y_sample"][0].rearrange("(t p) d -> p t d", p=P), x[:, 1:5, :]).then_inc(*st.up())
            sp.wait_ge(*st.now())


_OUTS = [("y_prompt", (1, 128, 1024)), ("y_sample", (1, 512, 1024)), ("new_diff_k", (1, 1, 128, 2, 4, 64)),
         ("new_diff_v", (1, 1, 128, 4, 128)), ("new_s5", (1, 1, 2, 2, 32, 64)), ("new_win_k", (1, 1, 128, 2, 64)),
         ("new_win_v", (1, 1, 128, 2, 64))]
_PLAIN = ["x_prompt", "x_sample", "cache_diff_k", "cache_diff_v", "cache_win_k", "cache_win_v", "c", "c_ctx", "ada_w",
          "ada_b", "norm_mix", "norm_ffn", "even_w_in", "even_w_out", "s5_log_step", "s5_d", "s5_w_glu", "diff_q_norm",
          "diff_k_norm", "diff_lambda", "diff_sub_norm", "odd_w_in", "odd_w_out", "win_q_norm", "win_k_norm",
          "win_sink", "pool_w", "pool_scale", "peer_w_q", "peer_u", "peer_v"]


def kernel(**inputs):
    import numpy as _np
    import concourse.bacc as _bacc
    from concourse import mybir as _mybir
    from concourse.bass_utils import run_bass_kernel_spmd as _run

    nc = _bacc.Bacc("TRN2", target_bir_lowering=False, num_devices=1)
    host = {name: _np.asarray(inputs[name]) for name in _PLAIN}
    lam = [_np.asarray(inputs[n])[0].transpose(0, 2, 1).reshape(128, 1, 32) for n in ("s5_lam_re", "s5_lam_im")]
    host["s5_lam"] = _np.concatenate(lam, axis=1)
    b = [_np.asarray(inputs[n])[0].transpose(0, 2, 1, 3).reshape(128, 1, 32, 16) for n in ("s5_b_re", "s5_b_im")]
    host["s5_b"] = _np.concatenate(b, axis=1)
    c = [_np.asarray(inputs[n])[0].transpose(0, 3, 1, 2).reshape(128, 1, 32, 16) for n in ("s5_c_re", "s5_c_im")]
    host["s5_c"] = _np.concatenate(c, axis=1)
    host["state_s5"] = _np.asarray(inputs["state_s5"])[0, 0].transpose(0, 3, 1, 2).reshape(128, 2, 32)
    host["peer_sub_keys"] = _np.asarray(inputs["peer_sub_keys"]).transpose(0, 4, 1, 2, 3).reshape(2, 128, 16, 128)
    host["consts"], host["pool_bands"] = constants()

    arrays, ins, outs = {}, {}, {}
    for name, a in host.items():
        a = _np.ascontiguousarray(a)
        arrays[f"in_{name}_dram"] = a
        ins[name] = nc.dram_tensor(f"in_{name}_dram", a.shape, _mybir.dt.from_np(a.dtype), kind="ExternalInput").ap()
    for name, shape in _OUTS:
        outs[name] = nc.dram_tensor(f"out_{name}_dram", shape, _mybir.dt.float32, kind="ExternalOutput").ap()
    build(nc, ins, outs)
    r = _run(nc, [arrays], core_ids=[0])
    return tuple(r.results[0][f"out_{name}_dram"] for name, _ in _OUTS)
```

```python
import math
from contextlib import ExitStack

import numpy as np

import concourse.bass as bass
from concourse import mybir

F32 = mybir.dt.float32
BF16 = mybir.dt.bfloat16
U32 = mybir.dt.uint32
I32 = mybir.dt.int32
ALU = mybir.AluOpType
ACT = mybir.ActivationFunctionType
AX = mybir.AxisListType.X
AXY = mybir.AxisListType.XY

P = 128
D = 1024
KD = D // P
NT = 5
TOK = NT * P
HALF = 512
EPS = 1e-6
G = 32
CH = 16
S = 8
NCH = TOK // S
NCP = P // S
DK = 64
SCALE = DK ** -0.5
LAM_INIT = 0.8 - 0.6 * math.exp(0.0)
EVEN_IN = 2048
ODD_IN = 1280
EXPERTS = 16384
TOPK = 16
HEADS = 8
HK = HEADS * TOPK
RING = 8
ROUNDS = HK // RING
PE_ROWS = (0, 2, 4, 6)
DVE_ROWS = (1, 3, 5, 7)
DIAGS = len(PE_ROWS)
TWO_PI_HI = 6.28125
TWO_PI_LO = 2 * math.pi - 6.28125
MAGIC = 12582912.0
POOL_WINDOWS = (2, 4, 8, 16)
BANKS = 6
PROMPT, SAMPLE = [0], [1, 2, 3, 4]


class Count:

    def __init__(self, sem, step=1):
        self.sem, self.step, self.n = sem, step, 0

    def up(self):
        self.n += self.step
        return self.sem, self.step

    def now(self):
        return self.sem, self.n


def constants():
    ident = np.eye(P, dtype=np.float32)
    iota = np.tile(np.arange(16, dtype=np.float32), (P, 1))
    pos = np.arange(512)
    freqs = (np.float32(10000.0) ** (-np.arange(16, dtype=np.float32) / np.float32(16))).astype(np.float32)
    ang = np.stack([(pos // 64).astype(np.float32)[:, None] * freqs,
                    (pos % 64).astype(np.float32)[:, None] * freqs], axis=1)
    c, s = np.cos(ang).astype(np.float32), np.sin(ang).astype(np.float32)
    cos = np.stack([c, c], axis=2).reshape(4, P, DK).transpose(1, 0, 2).reshape(P, -1)
    sin = np.stack([-s, s], axis=2).reshape(4, P, DK).transpose(1, 0, 2).reshape(P, -1)
    q, k = np.arange(P)[:, None], np.arange(P)[None, :]
    before = np.where(k >= q, 0.0, -1e30).astype(np.float32)
    after = np.where(k <= q, 0.0, -1e30).astype(np.float32)
    small = np.concatenate([ident, iota, cos, sin, before, after], axis=1)

    pool = np.zeros((P, 6, 4, P), np.float32)
    for w, wl in enumerate(POOL_WINDOWS):
        def band(length, t0, s0):
            t = np.arange(t0, t0 + P)[None, :]
            src = np.arange(s0, s0 + P)[:, None]
            lo, hi = np.clip(t - wl // 2, 0, length), np.clip(t + wl - wl // 2, 0, length)
            return ((src >= lo) & (src < hi)) / (hi - lo).astype(np.float32) - (src == t)
        pool[:, 0, w] = band(128, 0, 0)
        pool[:, 1, w] = band(512, 0, 0)
        pool[:, 2, w] = band(512, 128, 128)
        pool[:, 3, w] = band(512, 384, 384)
        pool[:, 4, w] = band(512, 128, 0)
        pool[:, 5, w] = band(512, 128, 256)
    return np.ascontiguousarray(small, np.float32), np.ascontiguousarray(pool.reshape(P, -1), np.float32)


CONSTS = 128 + 16 + 256 + 256 + 128 + 128


def build(nc, I, O):
    with ExitStack() as ctx:
        def sem(name):
            return ctx.enter_context(nc.semaphore(name))

        def count(name, step=1):
            return Count(sem(name), step)

        SIZES = dict(X=5120, H=5120, RING=RING * D, MOD=3072, GATES=2048, HT=4096, W=8192, Z=8192, PEER=2700,
                     TMP=4486, CONST=CONSTS, SMALL=600)
        arena = ctx.enter_context(nc.sbuf_tensor("arena", [P, sum(SIZES.values())], F32))
        at, off = {}, 0
        for name, size in SIZES.items():
            at[name] = off
            off += size

        def view(name, start, size, parts=P):
            return arena[0:parts, at[name] + start:at[name] + start + size]

        x = view("X", 0, 5120).rearrange("p (t d) -> p t d", t=NT)
        h = view("H", 0, 5120).rearrange("p (t d) -> p t d", t=NT)
        mod = view("MOD", 0, 3072).rearrange("p (m d) -> p m d", m=3)
        gates = view("GATES", 0, 2048).rearrange("p (c d) -> p c d", c=2)
        hT = view("HT", 0, 4096).rearrange("p (k t) -> p k t", k=KD)
        wbuf = view("W", 0, 8192).rearrange("p (s n) -> p s n", s=2)
        ident = view("CONST", 0, 128)
        iota16 = view("CONST", 128, 16)
        rope_c = view("CONST", 144, 256).rearrange("p (t d) -> p t d", t=4)
        rope_s = view("CONST", 400, 256).rearrange("p (t d) -> p t d", t=4)
        mask_before = view("CONST", 656, 128)
        mask_after = view("CONST", 784, 128)
        mask_both = view("CONST", 656, 256).rearrange("p (c k) -> p c k", c=2)
        ps = ctx.enter_context(nc.psum_tensor("ps", [P, 8, 512], F32))

        mod_dram = nc.dram_tensor("mod_rows", [2, 2, 6144], F32, kind="Internal").ap()
        bst_dram = nc.dram_tensor("s5_in", [2, P, G * P], F32, kind="Internal").ap()
        ca_dram = nc.dram_tensor("s5_out", [2, P, G * P], F32, kind="Internal").ap()
        kt_dram = nc.dram_tensor("s5_taps", [CH, G, 240], F32, kind="Internal").ap()

        block = ctx.enter_context(nc.Block())
        dve_did, act_did, pe_did, pool_did = count("dve_did"), count("act_did"), count("pe_did"), count("pool_did")
        full = [sem(f"bank_full{b}") for b in range(BANKS)]
        free = [sem(f"bank_free{b}") for b in range(BANKS)]
        w_in = [count(f"weights_in{s}", 16) for s in range(2)]
        dma_groups = []

        def group(name):
            dma_groups.append(count(f"{name}_{len(dma_groups)}", 16))
            return dma_groups[-1]
        w_last = [[], []]
        state = dict(items=0, w=0)

        def link(eng, did, ins):
            ins.then_inc(*did.up())
            eng.wait_ge(*did.now())

        def take(n):
            first = state["items"]
            state["items"] += n
            return first

        def bank(i):
            return ps[:, i % BANKS, :]

        def open_bank(pe, i):
            if i >= BANKS:
                pe.wait_ge(free[i % BANKS], i // BANKS)

        def filled(i):
            return full[i % BANKS], i // BANKS + 1

        def emptied(i):
            return free[i % BANKS], i // BANKS + 1

        def fills(i):
            return full[i % BANKS], 1

        def empties(i):
            return free[i % BANKS], 1

        def last_emptied(i, n=BANKS):
            return [emptied(k) for k in range(max(0, i - n + 1), i + 1)]

        def load_weights(src, shape_of, after=()):
            slot = state["w"] % 2
            state["w"] += 1
            dst = shape_of(wbuf[:, slot, :])

            @block.sync
            def _(sp):
                for mark in list(after) + w_last[slot]:
                    sp.wait_ge(*mark)
                sp.dma_start(dst, src).then_inc(*w_in[slot].up())
            return slot, dst, w_in[slot].now()

        met = {name: {} for name in "tvsy"}

        def meet(engines="tvsy"):
            marks = [c.now() for c in (dve_did, act_did, pe_did, *dma_groups, w_in[0], w_in[1]) if c.n]
            marks += last_emptied(state["items"] - 1) if state["items"] else []

            def wait(eng, name):
                for which, value in marks:
                    if met[name].get(which, 0) < value:
                        met[name][which] = value
                        eng.wait_ge(which, value)
            if "t" in engines:
                @block.tensor
                def _(pe):
                    wait(pe, "t")
            if "v" in engines:
                @block.vector
                def _(dve):
                    wait(dve, "v")
            if "s" in engines:
                @block.scalar
                def _(act):
                    wait(act, "s")
            if "y" in engines:
                @block.sync
                def _(sp):
                    wait(sp, "y")

        cond = view("SMALL", 0, 16).rearrange("p (j c) -> p j c", c=2)
        cond_sig = view("SMALL", 16, 16).rearrange("p (j c) -> p j c", c=2)
        ones2 = view("SMALL", 32, 2)
        a8_re = view("SMALL", 34, 32)
        a8_im = view("SMALL", 66, 32)
        a8_nim = view("SMALL", 98, 32)
        neg_lam = view("SMALL", 130, 1)
        sink_col = view("SMALL", 131, 8)
        stat = view("SMALL", 139, 128)
        pscale_col = view("SMALL", 270, 4)
        stat2 = view("SMALL", 280, 128)
        zero_w = view("SMALL", 408, 64).bitcast(BF16)
        state0 = view("SMALL", 472, 64)
        lv_row = view("PEER", 6688, 256)

        ld = group("loads_in")
        @block.sync
        def _(sp):
            sp.dma_start(view("CONST", 0, CONSTS), I["consts"]).then_inc(*ld.up())
            with nc.allow_non_contiguous_dma(reason="two conditioning columns"):
                sp.dma_start(cond[:, :, 0], I["c_ctx"].rearrange("(p j) -> p j", j=8)).then_inc(*ld.up())
                sp.dma_start(cond[:, :, 1], I["c"][0].rearrange("(p j) -> p j", j=8)).then_inc(*ld.up())
        cond_in = ld.now()
        @block.scalar
        def _(act):
            act.wait_ge(*cond_in)
            nc.scalar.activation(cond_sig, cond, ACT.Sigmoid).then_inc(*act_did.up())
        sig_ready = act_did.now()

        @block.vector
        def _(dve):
            nc.vector.memset(ones2, 1.0).then_inc(*dve_did.up())
            nc.vector.memset(zero_w, 0.0).then_inc(*dve_did.up())
            dve.wait_ge(*sig_ready)
            nc.vector.tensor_tensor(cond, cond, cond_sig, ALU.mult).then_inc(*dve_did.up())
        cond_ready = dve_did.now()

        def ada(l, which, beside=False):
            bias, row = (view("MOD", 0, 3072, 1), view("GATES", 0, 3072, 1))[which], view("Z", 3072 * which, 3072, 2)
            if not beside:
                bias = view("MOD", 0, 3072, 1)
                meet()
            ld = group("ada_bias_in")

            @block.sync
            def _(sp):
                sp.dma_start(bias, I["ada_b"][l:l + 1, which * 3072:(which + 1) * 3072]).then_inc(*ld.up())
            bias_in = ld.now()
            w_rows = I["ada_w"][l].rearrange("(p j) n -> p j n", j=8)
            for blk in range(6):
                col = which * 3072 + blk * 512
                slot, w, w_mark = load_weights(w_rows[:, :, col:col + 512], lambda a: a.rearrange("p (j n) -> p j n", j=8))
                i = take(1)
                w_last[slot] = [filled(i)]

                @block.tensor
                def _(pe):
                    open_bank(pe, i)
                    pe.wait_ge(*w_mark)
                    if blk == 0:
                        pe.wait_ge(*cond_ready)
                        pe.wait_ge(*bias_in)
                    for j in range(8):
                        nc.tensor.matmul(bank(i)[0:2, :], cond[:, j, :], w[:, j, :], start=(j == 0), stop=False)
                    nc.tensor.matmul(bank(i)[0:2, :], ones2[0:1, :], bias[:, blk * 512:(blk + 1) * 512],
                                     start=False, stop=True).then_inc(*fills(i))

                @block.scalar
                def _(act):
                    act.wait_ge(*filled(i))
                    nc.scalar.copy(row[:, blk * 512:(blk + 1) * 512], bank(i)[0:2, :]).then_inc(*empties(i))
                yield
            st = group("ada_rows_out")

            @block.sync
            def _(sp):
                for m in last_emptied(i):
                    sp.wait_ge(*m)
                sp.dma_start(mod_dram[l, :, which * 3072:(which + 1) * 3072], row).then_inc(*st.up())
            yield

        def pv(start, size):
            return view("PEER", start, size)
        lam = pv(0, 64).rearrange("p (r g) -> p r g", r=2)
        step = pv(64, 32)
        arg = pv(96, 64).rearrange("p (r g) -> p r g", r=2)
        mag = pv(160, 32)
        trig = pv(192, 64).rearrange("p (r g) -> p r g", r=2)
        den = pv(256, 32)
        fac = pv(288, 64).rearrange("p (r g) -> p r g", r=2)
        t32 = pv(352, 128).rearrange("p (n g) -> p n g", n=4)
        pw = pv(480, 576).rearrange("p (r k g) -> p r k g", r=2, k=9)
        pb = pv(1056, 512).rearrange("p (r s g) -> p r s g", r=2, s=8)
        pc = pv(1568, 512).rearrange("p (r s g) -> p r s g", r=2, s=8)
        braw = pv(2080, 1024).rearrange("p (r g c) -> p r g c", r=2, c=CH)
        bbar = pv(3104, 1024).rearrange("p (r g c) -> p r g c", r=2, c=CH)
        tmp = pv(4640, 512).rearrange("p (g c) -> p g c", c=CH)
        tmp2 = pv(5152, 512).rearrange("p (g c) -> p g c", c=CH)
        craw = pv(5664, 1024).rearrange("p (r g c) -> p r g c", r=2, c=CH)
        ncim = pv(4128, 512).rearrange("p (g c) -> p g c", c=CH)
        BB = [view("RING", 0, 4096).rearrange("p (g s c) -> p g s c", g=G, s=S),
              view("RING", 4096, 4096).rearrange("p (g s c) -> p g s c", g=G, s=S)]
        CA = [arena[:, at["X"] + r * 4096:at["X"] + (r + 1) * 4096].rearrange("p (g s c) -> p g s c", g=G, s=S)
              for r in range(2)]

        ld = group("loads_in")
        @block.sync
        def _(sp):
            sp.dma_start(lam, I["s5_lam"]).then_inc(*ld.up())
            for d in range(2):
                sp.dma_start(step[64 * d:64 * d + 64, :], I["s5_log_step"][0, d:d + 1, :].to_broadcast([64, G])
                             ).then_inc(*ld.up())
            sp.dma_start(braw, I["s5_b"]).then_inc(*ld.up())
            sp.dma_start(craw, I["s5_c"]).then_inc(*ld.up())
            sp.dma_start(lv_row, I["diff_lambda"].rearrange("a b d -> a (b d)").to_broadcast([P, 256])).then_inc(*ld.up())
        s5_in = ld.now()

        @block.scalar
        def _(act):
            act.wait_ge(*s5_in)
            nc.scalar.activation(step, step, ACT.Exp).then_inc(*act_did.up())
        step_ready = act_did.now()

        @block.vector
        def _(dve):
            dve.wait_ge(*step_ready)
            v = nc.vector
            link(dve, dve_did, v.tensor_tensor(arg, lam, step.unsqueeze(1).to_broadcast([P, 2, G]), ALU.mult))
            link(dve, dve_did, v.tensor_scalar(t32[:, 0], arg[:, 1], 1 / (2 * math.pi), MAGIC, ALU.mult, ALU.add))
            link(dve, dve_did, v.tensor_scalar(t32[:, 0], t32[:, 0], -MAGIC, None, ALU.add))
            link(dve, dve_did, v.scalar_tensor_tensor(t32[:, 1], t32[:, 0], -TWO_PI_HI, arg[:, 1], ALU.mult, ALU.add))
            link(dve, dve_did, v.scalar_tensor_tensor(t32[:, 1], t32[:, 0], -TWO_PI_LO, t32[:, 1], ALU.mult, ALU.add))
            link(dve, dve_did, v.tensor_scalar(t32[:, 2], t32[:, 1], 0.0, None, ALU.is_gt))
            link(dve, dve_did, v.tensor_scalar(t32[:, 2], t32[:, 2], -2.0, 1.0, ALU.mult, ALU.add))
            link(dve, dve_did, v.tensor_tensor(t32[:, 2], t32[:, 1], t32[:, 2], ALU.mult))
            link(dve, dve_did, v.tensor_scalar(t32[:, 2], t32[:, 2], math.pi / 2, None, ALU.add))
            link(dve, dve_did, v.tensor_scalar(t32[:, 1], t32[:, 1], 3.1415925, -3.1415925, ALU.min, ALU.max))
        arg_ready = dve_did.now()

        @block.scalar
        def _(act):
            act.wait_ge(*arg_ready)
            nc.scalar.activation(mag, arg[:, 0], ACT.Exp).then_inc(*act_did.up())
            nc.scalar.activation(trig[:, 0], t32[:, 2], ACT.Sin).then_inc(*act_did.up())
            nc.scalar.activation(trig[:, 1], t32[:, 1], ACT.Sin).then_inc(*act_did.up())
        trig_ready = act_did.now()

        @block.vector
        def _(dve):
            v = nc.vector

            def L(ins):
                link(dve, dve_did, ins)

            def cmul(o_re, o_im, a_re, a_im, b_re, b_im, u, w):
                L(v.tensor_tensor(u, a_re, b_re, ALU.mult))
                L(v.tensor_tensor(w, a_im, b_im, ALU.mult))
                L(v.tensor_tensor(o_re, u, w, ALU.subtract))
                L(v.tensor_tensor(u, a_re, b_im, ALU.mult))
                L(v.tensor_tensor(w, a_im, b_re, ALU.mult))
                L(v.tensor_tensor(o_im, u, w, ALU.add))

            dve.wait_ge(*trig_ready)
            L(v.memset(pw[:, 0, 0], 1.0))
            L(v.memset(pw[:, 1, 0], 0.0))
            L(v.tensor_tensor(pw[:, 0, 1], mag, trig[:, 0], ALU.mult))
            L(v.tensor_tensor(pw[:, 1, 1], mag, trig[:, 1], ALU.mult))
            for k in range(2, 9):
                cmul(pw[:, 0, k], pw[:, 1, k], pw[:, 0, k - 1], pw[:, 1, k - 1], pw[:, 0, 1], pw[:, 1, 1],
                     t32[:, 0], t32[:, 1])
            L(v.tensor_copy(a8_re, pw[:, 0, 8]))
            L(v.tensor_copy(a8_im, pw[:, 1, 8]))
            L(v.tensor_scalar(a8_nim, pw[:, 1, 8], -1.0, None, ALU.mult))
            L(v.tensor_copy(pb[0:64], pw[0:64, :, 7::-1, :]))
            L(v.tensor_copy(pb[64:128], pw[64:128, :, 0:8, :]))
            L(v.tensor_copy(pc[0:64], pw[0:64, :, 1:9, :]))
            L(v.tensor_copy(pc[64:128], pw[64:128, :, 8:0:-1, :]))
            L(v.tensor_tensor(t32[:, 0], lam[:, 0], lam[:, 0], ALU.mult))
            L(v.tensor_tensor(t32[:, 1], lam[:, 1], lam[:, 1], ALU.mult))
            L(v.tensor_tensor(den, t32[:, 0], t32[:, 1], ALU.add))
            L(v.reciprocal(den, den))
            L(v.tensor_scalar(t32[:, 2], pw[:, 0, 1], -1.0, None, ALU.add))
            L(v.tensor_scalar(t32[:, 3], lam[:, 1], -1.0, None, ALU.mult))
            cmul(fac[:, 0], fac[:, 1], t32[:, 2], pw[:, 1, 1], lam[:, 0], t32[:, 3], t32[:, 0], t32[:, 1])
            L(v.tensor_tensor(fac, fac, den.unsqueeze(1).to_broadcast([P, 2, G]), ALU.mult))

            def over_c(a):
                return a.unsqueeze(2).to_broadcast([P, G, CH])
            cmul(bbar[:, 0], bbar[:, 1], braw[:, 0], braw[:, 1], over_c(fac[:, 0]), over_c(fac[:, 1]), tmp, tmp2)
            L(v.tensor_scalar(ncim, craw[:, 1], -1.0, None, ALU.mult))
            for s in range(S):
                cmul(BB[0][:, :, s, :], BB[1][:, :, s, :], bbar[:, 0], bbar[:, 1],
                     over_c(pb[:, 0, s]), over_c(pb[:, 1, s]), tmp, tmp2)
            for s in range(S):
                cmul(CA[0][:, :, s, :], CA[1][:, :, s, :], craw[:, 0], craw[:, 1],
                     over_c(pc[:, 0, s]), over_c(pc[:, 1, s]), tmp, tmp2)
                L(v.tensor_scalar(CA[1][:, :, s, :], CA[1][:, :, s, :], -1.0, None, ALU.mult))
            L(v.tensor_tensor(lv_row[:, 0:64], lv_row[:, 0:64], lv_row[:, 64:128], ALU.mult))
            L(v.tensor_tensor(lv_row[:, 128:192], lv_row[:, 128:192], lv_row[:, 192:256], ALU.mult))
            L(v.tensor_reduce(stat[:, 0:1], lv_row[:, 0:64], AX, ALU.add))
            L(v.tensor_reduce(stat[:, 1:2], lv_row[:, 128:192], AX, ALU.add))
        tables_ready = dve_did.now()
        for which in range(2):
            for _ in ada(0, which, beside=True):
                pass

        @block.scalar
        def _(act):
            act.wait_ge(*tables_ready)
            nc.scalar.activation(stat[:, 0:2], stat[:, 0:2], ACT.Exp).then_inc(*act_did.up())
        lam_exp = act_did.now()

        @block.vector
        def _(dve):
            dve.wait_ge(*lam_exp)
            link(dve, dve_did, nc.vector.tensor_tensor(neg_lam, stat[:, 1:2], stat[:, 0:1], ALU.subtract))
            link(dve, dve_did, nc.vector.tensor_scalar(neg_lam, neg_lam, -LAM_INIT, None, ALU.add))

        bst = view("HT", 0, 4096).rearrange("p (g m) -> p g m", g=G)
        for r in range(2):
            i0 = take(8)
            out_before = st.now() if r else None

            @block.tensor
            def _(pe):
                pe.wait_ge(*tables_ready)
                for n in range(8):
                    open_bank(pe, i0 + n)
                    for q in range(4):
                        g = 4 * n + q
                        ins = nc.tensor.transpose(bank(i0 + n)[:, q * P:(q + 1) * P],
                                                  BB[r][:, g].rearrange("p s c -> p (s c)"), ident)
                    ins.then_inc(*fills(i0 + n))

            @block.scalar
            def _(act):
                if r:
                    act.wait_ge(*out_before)
                for n in range(8):
                    act.wait_ge(*filled(i0 + n))
                    nc.scalar.copy(bst[:, 4 * n:4 * n + 4, :].rearrange("p g m -> p (g m)"), bank(i0 + n)).then_inc(*empties(i0 + n))

            st = group("stores_out")
            @block.sync
            def _(sp):
                for m in last_emptied(i0 + 7):
                    sp.wait_ge(*m)
                sp.dma_start(bst_dram[r], bst.rearrange("p g m -> p (g m)")).then_inc(*st.up())
                sp.wait_ge(*tables_ready)
                sp.dma_start(ca_dram[r], CA[r].rearrange("p g s c -> p (g s c)")).then_inc(*st.up())

        taps = view("Z", 0, G * 240, CH).rearrange("p (g o) -> p g o", g=G)
        meet("s")
        i0 = take(17)
        lo, hi = slice(0, 64), slice(64, 128)

        def ca(r, rows, g, j0):
            return CA[r][rows, g, j0:j0 + 7, :].rearrange("p s c -> p (s c)")

        @block.tensor
        def _(pe):
            for n in range(16):
                rows, j0 = (lo, 0) if n < 8 else (hi, 1)
                open_bank(pe, i0 + n)
                for q in range(4):
                    g = 4 * (n % 8) + q
                    for r in range(2):
                        ins = nc.tensor.matmul(bank(i0 + n)[0:CH, 112 * q:112 * q + 112], bbar[rows, r, g], ca(r, rows, g, j0),
                                               start=(r == 0), stop=(r == 1))
                ins.then_inc(*fills(i0 + n))
            open_bank(pe, i0 + 16)
            for g in range(G):
                o = bank(i0 + 16)[0:CH, CH * g:CH * g + CH]
                nc.tensor.matmul(o, bbar[:, 0, g], craw[:, 0, g], start=True, stop=False)
                ins = nc.tensor.matmul(o, bbar[:, 1, g], ncim[:, g], start=False, stop=True)
            ins.then_inc(*fills(i0 + 16))

        @block.scalar
        def _(act):
            for n in range(17):
                act.wait_ge(*filled(i0 + n))
                g, o = 4 * (n % 8), 128 if n < 8 else 0
                dst = taps[:, g:g + 4, o:o + 112] if n < 16 else taps[:, :, 112:128]
                src = bank(i0 + n)[0:CH, 0:448].rearrange("p (g o) -> p g o", g=4) if n < 16 else \
                    bank(i0 + n)[0:CH, :].rearrange("p (g o) -> p g o", g=G)
                nc.scalar.copy(dst, src).then_inc(*empties(i0 + n))

        st = group("stores_out")
        @block.sync
        def _(sp):
            for m in last_emptied(i0 + 16):
                sp.wait_ge(*m)
            sp.dma_start(kt_dram, taps).then_inc(*st.up())
        meet()

        ld = group("loads_in")
        @block.sync
        def _(sp):
            sp.dma_start(x[:, 0, :], I["x_prompt"][0]).then_inc(*ld.up())
            sp.dma_start(x[:, 1:5, :], I["x_sample"][0].rearrange("(t p) d -> p t d", p=P)).then_inc(*ld.up())

        pace = [1]

        def modulate(l, which, tiles, norm, part=None):
            part = part or tiles
            first = part[0] == tiles[0]
            c = min(tiles[0], 1)
            norm_row = view("TMP", 0, 1024)
            n_t = len(part)
            meet()
            ld = group("modulation_in")

            @block.sync
            def _(sp):
                if not first:
                    return
                sp.dma_start(mod.rearrange("p m d -> p (m d)"),
                             mod_dram[l, c:c + 1, which * 3072:(which + 1) * 3072].to_broadcast([P, 3072])).then_inc(*ld.up())
                sp.dma_start(norm_row, norm[l:l + 1, :].to_broadcast([P, D])).then_inc(*ld.up())
            mods_in = ld.now()

            @block.scalar
            def _(act):
                for n, t in enumerate(part):
                    nc.scalar.activation(h[:, t], x[:, t], ACT.Square, accum_out=stat[:, n:n + 1]).then_inc(*act_did.up())
            squares = act_did.now()

            @block.vector
            def _(dve):
                dve.wait_ge(*squares)
                link(dve, dve_did, nc.vector.tensor_scalar(stat[:, 0:n_t], stat[:, 0:n_t], 1.0 / D, EPS, ALU.mult, ALU.add))
            var_ready = dve_did.now()

            @block.scalar
            def _(act):
                act.wait_ge(*var_ready)
                nc.scalar.activation(stat[:, 8:8 + n_t], stat[:, 0:n_t], ACT.Sqrt).then_inc(*act_did.up())
            std_ready = act_did.now()

            @block.vector
            def _(dve):
                if first:
                    dve.wait_ge(*mods_in)
                    nc.vector.scalar_tensor_tensor(mod[:, 1], mod[:, 1], 1.0, norm_row, ALU.add, ALU.mult).then_inc(*dve_did.up())
                if which:
                    nc.vector.tensor_copy(gates[:, c], mod[:, 2]).then_inc(*dve_did.up())
                dve.wait_ge(*std_ready)
                link(dve, dve_did, nc.vector.reciprocal(stat[:, 16:16 + n_t], stat[:, 8:8 + n_t]))
            yield
            for n, t in enumerate(part):
                column = (t - tiles[0]) * P

                @block.vector
                def _(dve):
                    link(dve, dve_did, nc.vector.scalar_tensor_tensor(h[:, t], x[:, t], stat[:, 16 + n:17 + n], mod[:, 1], ALU.mult, ALU.mult))
                    nc.vector.tensor_tensor(h[:, t], h[:, t], mod[:, 0], ALU.add).then_inc(*dve_did.up())
                tile_ready = dve_did.now()
                i0 = take(2)

                @block.tensor
                def _(pe):
                    pe.wait_ge(*tile_ready)
                    for b in range(2):
                        open_bank(pe, i0 + b)
                        for q in range(4):
                            ins = nc.tensor.transpose(bank(i0 + b)[:, q * P:(q + 1) * P], h[:, t, (4 * b + q) * P:(4 * b + q + 1) * P], ident)
                        ins.then_inc(*fills(i0 + b))

                @block.scalar
                def _(act):
                    for b in range(2):
                        act.wait_ge(*filled(i0 + b))
                        nc.scalar.copy(hT[:, 4 * b:4 * b + 4, column:column + P],
                                       bank(i0 + b).rearrange("p (q t) -> p q t", q=4)).then_inc(*empties(i0 + b))
                yield
            return last_emptied(i0 + 1)

        def project(w_dram, col0, ncols, places, dst, ready):
            slot, w, w_mark = load_weights(w_dram.rearrange("(k p) n -> p k n", p=P)[:, :, col0:col0 + ncols],
                                           lambda a: a[:, 0:8 * ncols].rearrange("p (k n) -> p k n", k=KD))
            for n in places:
                i = take(1)
                w_last[slot] = [filled(i)]

                @block.tensor
                def _(pe):
                    if n == places[0]:
                        for m in ready:
                            pe.wait_ge(*m)
                        pe.wait_ge(*w_mark)
                    open_bank(pe, i)
                    for k in range(KD):
                        ins = nc.tensor.matmul(bank(i)[:, 0:ncols], hT[:, k, n * P:(n + 1) * P], w[:, k, :],
                                               start=(k == 0), stop=(k == KD - 1))
                    ins.then_inc(*fills(i))

                @block.scalar
                def _(act):
                    act.wait_ge(*filled(i))
                    nc.scalar.copy(dst(n), bank(i)[:, 0:ncols]).then_inc(*empties(i))
                yield
            return last_emptied(i)

        def transposes(srcs, dst_of, ready):
            for n, blocks in enumerate(srcs):
                i = take(1)
                k = blocks[0].shape[0]

                @block.tensor
                def _(pe):
                    if n == 0:
                        for m in ready:
                            pe.wait_ge(*m)
                    open_bank(pe, i)
                    for q, src in enumerate(blocks):
                        ins = nc.tensor.transpose(bank(i)[:, q * P:q * P + k], src, ident[0:k, 0:k])
                    ins.then_inc(*fills(i))

                @block.scalar
                def _(act):
                    act.wait_ge(*filled(i))
                    src = bank(i)[:, 0:len(blocks) * P].rearrange("p (q t) -> p q t", t=P)[:, :, 0:k]
                    nc.scalar.copy(dst_of(n), src).then_inc(*empties(i))
                yield
            return last_emptied(i)

        def qk_norm_rope(z, tiles, gains, tmp_sq, ready):
            g = sum(k for k, _ in gains)
            width = g * DK
            for n, t in enumerate(tiles):
                zt = z(n)[:, 0:width].rearrange("p (g d) -> p g d", d=DK)
                sq = tmp_sq[:, 0:width].rearrange("p (g d) -> p g d", d=DK)

                @block.vector
                def _(dve):
                    for m in ready:
                        dve.wait_ge(*m)
                    link(dve, dve_did, nc.vector.tensor_tensor(sq, zt, zt, ALU.mult))
                    link(dve, dve_did, nc.vector.tensor_reduce(stat[:, 0:g], sq, AX, ALU.add))
                    link(dve, dve_did, nc.vector.tensor_scalar(stat[:, 0:g], stat[:, 0:g], 1.0 / DK, EPS, ALU.mult, ALU.add))
                var_ready = dve_did.now()

                @block.scalar
                def _(act):
                    act.wait_ge(*var_ready)
                    nc.scalar.activation(stat[:, 16:16 + g], stat[:, 0:g], ACT.Sqrt).then_inc(*act_did.up())
                std_ready = act_did.now()
                yield

                @block.vector
                def _(dve):
                    dve.wait_ge(*std_ready)
                    link(dve, dve_did, nc.vector.reciprocal(stat[:, 32:32 + g], stat[:, 16:16 + g]))
                    link(dve, dve_did, nc.vector.tensor_tensor(zt, zt, stat[:, 32:32 + g].unsqueeze(2).to_broadcast([P, g, DK]), ALU.mult))
                    g0 = 0
                    for k, row in gains:
                        nc.vector.tensor_tensor(zt[:, g0:g0 + k], zt[:, g0:g0 + k], row.unsqueeze(1).to_broadcast([P, k, DK]),
                                                ALU.mult).then_inc(*dve_did.up())
                        g0 += k
                    dve.wait_ge(*dve_did.now())
                    if t:
                        z4 = z(n)[:, 0:width].rearrange("p (g a b) -> p g a b", a=2, b=32)
                        s4 = tmp_sq[:, 0:width].rearrange("p (g a b) -> p g a b", a=2, b=32)
                        c_t = rope_c[:, t - 1].unsqueeze(1).to_broadcast([P, g, DK])
                        s_t = rope_s[:, t - 1].rearrange("p (a b) -> p a b", a=2)
                        for half in range(2):
                            o, i = 16 * half, 16 - 16 * half
                            nc.vector.tensor_tensor(s4[:, :, :, o:o + 16], z4[:, :, :, i:i + 16],
                                                    s_t[:, :, o:o + 16].unsqueeze(1).to_broadcast([P, g, 2, 16]),
                                                    ALU.mult).then_inc(*dve_did.up())
                        dve.wait_ge(*dve_did.now())
                        link(dve, dve_did, nc.vector.tensor_tensor(zt, zt, c_t, ALU.mult))
                        link(dve, dve_did, nc.vector.tensor_tensor(zt, zt, sq, ALU.add))
                yield
            return [dve_did.now()]

        def add_gated(dve, t, half, src, marks, gate_row, tmp512):
            cols = slice(half * 512, (half + 1) * 512)
            nc.vector.tensor_tensor(tmp512, src, gate_row[:, cols], ALU.mult).then_inc(*marks)
            link(dve, dve_did, nc.vector.memset(stat2[:, 127:128], 0.0))
            link(dve, dve_did, nc.vector.tensor_tensor(x[:, t, cols], x[:, t, cols], tmp512, ALU.add))

        def out_project(w_dram, tiles, cat, ready):
            for half in range(2):
                slot, w, w_mark = load_weights(w_dram.rearrange("(k p) n -> p k n", p=P)[:, :, half * 512:(half + 1) * 512],
                                               lambda a: a.rearrange("p (k n) -> p k n", k=KD))
                for n, t in enumerate(tiles):
                    i = take(1)
                    w_last[slot] = [filled(i)]

                    @block.tensor
                    def _(pe):
                        if n == 0:
                            for m in ready:
                                pe.wait_ge(*m)
                            pe.wait_ge(*w_mark)
                        open_bank(pe, i)
                        for k in range(KD):
                            ins = nc.tensor.matmul(bank(i), cat(k)[:, n * P:(n + 1) * P], w[:, k, :], start=(k == 0), stop=(k == KD - 1))
                        ins.then_inc(*fills(i))

                    @block.vector
                    def _(dve):
                        dve.wait_ge(*filled(i))
                        add_gated(dve, t, half, bank(i), empties(i), mod[:, 2], view("TMP", 0, 512))
                    yield

        s_scan, scan_granted = sem("scan_steps"), sem("scan_products_seen")
        scan_count = [0]

        def aux(tiles, start, size, parts=P):
            if tiles == SAMPLE:
                return arena[0:parts, at["H"] + D + start:at["H"] + D + start + size]
            return view("Z", 5120 + start, size, parts)

        def s5(tiles, hT_ready, beside_scan=None):
            T = len(tiles) * P
            n_ch = T // S
            prompt = tiles == PROMPT
            u_c = view("Z", 0, 4096, n_ch).rearrange("p (g s c) -> p g s c", g=G, s=S)
            slot, w, w_mark = load_weights(I["even_w_in"][0].rearrange("(k p) n -> p k n", p=P)[:, :, 0:512],
                                           lambda a: a.rearrange("p (k n) -> p k n", k=KD))
            for s in range(S):
                i = take(1)
                w_last[slot] = [filled(i)]

                @block.tensor
                def _(pe):
                    if s == 0:
                        for m in hT_ready:
                            pe.wait_ge(*m)
                        pe.wait_ge(*w_mark)
                    open_bank(pe, i)
                    for k in range(KD):
                        ins = nc.tensor.matmul(bank(i)[0:n_ch, :], hT[:, k, s:T:S], w[:, k, :], start=(k == 0), stop=(k == KD - 1))
                    ins.then_inc(*fills(i))

                @block.scalar
                def _(act):
                    act.wait_ge(*filled(i))
                    nc.scalar.copy(u_c[:, :, s, :], bank(i)[0:n_ch, :].rearrange("p (g c) -> p g c", g=G)).then_inc(*empties(i))
                yield
            u_ready = last_emptied(i)

            xg = view("Z", 4096, G * n_ch).rearrange("p (g n) -> p g n", g=G)
            for b in range(4):
                i = take(1)

                @block.tensor
                def _(pe):
                    if b == 0:
                        for m in u_ready:
                            pe.wait_ge(*m)
                    open_bank(pe, i)
                    for q in range(8):
                        ins = nc.tensor.transpose(bank(i)[:, q * n_ch:(q + 1) * n_ch], u_c[:, 8 * b + q].rearrange("p s c -> p (s c)"),
                                                  ident[0:n_ch, 0:n_ch])
                    ins.then_inc(*fills(i))

                @block.scalar
                def _(act):
                    act.wait_ge(*filled(i))
                    nc.scalar.copy(xg[:, 8 * b:8 * b + 8, :].rearrange("p g n -> p (g n)"), bank(i)[:, 0:8 * n_ch]).then_inc(*empties(i))
                yield
            xg_ready = last_emptied(i)

            hs = view("TMP", 0, 64 * n_ch).rearrange("p (r g k) -> p r g k", r=2, g=G)
            s5_d_row = (aux(tiles, 3584, 512, n_ch) if tiles == SAMPLE else view("Z", 4608, 512, n_ch))
            h0 = state0.rearrange("p (r g) -> p r g", r=2)
            meet("y")
            ld = group("s5_rows_in")

            @block.sync
            def _(sp):
                sp.dma_start(h0, I["state_s5"]).then_inc(*ld.up())
                sp.dma_start(s5_d_row, I["s5_d"].to_broadcast([n_ch, 512])).then_inc(*ld.up())
            rows_in = ld.now()
            for hf in range(2):
                slot, w, w_mark = load_weights(bst_dram.rearrange("r p (g m) -> p r g m", g=G)[:, :, 16 * hf:16 * hf + 16, :],
                                               lambda a: a.rearrange("p (r g m) -> p r g m", r=2, g=16))
                for b in range(4):
                    i = take(1)
                    r, g = b // 2, 8 * (b % 2)
                    w_last[slot] = [filled(i)]

                    @block.tensor
                    def _(pe):
                        if b == 0:
                            for m in xg_ready:
                                pe.wait_ge(*m)
                            pe.wait_ge(*w_mark)
                        open_bank(pe, i)
                        for q in range(8):
                            ins = nc.tensor.matmul(bank(i)[:, q * n_ch:(q + 1) * n_ch], w[:, r, g + q, :], xg[:, 16 * hf + g + q, :],
                                                   start=True, stop=True)
                        ins.then_inc(*fills(i))

                    @block.scalar
                    def _(act):
                        src = bank(i)[:, 0:8 * n_ch].rearrange("p (q n) -> p q n", q=8)
                        gg = 16 * hf + g
                        act.wait_ge(*filled(i))
                        nc.scalar.copy(hs[0:64, r, gg:gg + 8, :], src[0:64])
                        nc.scalar.copy(hs[64:128, r, gg:gg + 8, :], src[64:128, :, ::-1]).then_inc(*empties(i))
                    yield
            hs_ready = last_emptied(i) + [rows_in]

            hop = view("Z", 7040, 192).rearrange("p (n r g) -> p n r g", n=3, r=2)

            def scan_step(dve, before, cur, value):
                a_re = a8_re.unsqueeze(1).to_broadcast([P, 2, G])
                nc.vector.tensor_copy(hop[:, 2], cur)
                nc.vector.tensor_tensor(hop[:, 0], before, a_re, ALU.mult)
                nc.vector.tensor_tensor(hop[:, 1, 0], before[:, 1], a8_nim, ALU.mult)
                nc.vector.tensor_tensor(hop[:, 1, 1], before[:, 0], a8_im, ALU.mult).then_inc(s_scan, 1)
                dve.wait_ge(s_scan, value + 1)
                dve.sem_inc(scan_granted, 1)
                nc.vector.tensor_reduce(cur, hop.rearrange("p n r g -> p r g n"), AX, ALU.add).then_inc(s_scan, 1)
                dve.wait_ge(s_scan, value + 2)

            def col(k):
                return hs[:, :, :, bass.ds(k, 1)].rearrange("p r g k -> p r (g k)")

            @block.vector
            def _(dve):
                for m in hs_ready:
                    dve.wait_ge(*m)
                for m in xg_ready:
                    dve.wait_ge(*m)
                link(dve, dve_did, nc.vector.tensor_tensor(u_c, u_c, s5_d_row.rearrange("p (g c) -> p g c", g=G).unsqueeze(2).to_broadcast([n_ch, G, S, CH]), ALU.mult))
                if not prompt:
                    scan_step(dve, h0, hs[:, :, :, 0], scan_count[0])
                    scan_count[0] += 2
            first = 1
            while first < n_ch:
                k = min(5, n_ch - first)

                @block.vector
                def _(dve):
                    base = scan_count[0] - 2 * first
                    with dve.Fori(first, first + k) as c:
                        scan_step(dve, col(c - 1), col(c), c * 2 + base)
                scan_count[0] += 2 * k
                first += k
                if beside_scan is not None:
                    next(beside_scan, None)
                if first < n_ch:
                    yield
            scan_done = (s_scan, scan_count[0])

            if prompt:
                fin_in, fin_out = view("Z", 7296, 64), view("Z", 7424, 128, 64)

                @block.vector
                def _(dve):
                    link(dve, dve_did, nc.vector.tensor_copy(fin_in.rearrange("p (r g) -> p r g", r=2), hs[:, :, :, n_ch - 1]))
                fin_ready = dve_did.now()
                i = take(1)

                @block.tensor
                def _(pe):
                    open_bank(pe, i)
                    pe.wait_ge(*fin_ready)
                    nc.tensor.transpose(bank(i)[0:64, 0:P], fin_in, ident).then_inc(*fills(i))

                @block.scalar
                def _(act):
                    act.wait_ge(*filled(i))
                    nc.scalar.copy(fin_out, bank(i)[0:64, 0:P]).then_inc(*empties(i))
                st = group("final_states_out")

                @block.sync
                def _(sp):
                    sp.wait_ge(*emptied(i))
                    for d in range(2):
                        sp.dma_start(O["new_s5"][0, 0, d].rearrange("r g p -> (r g) p"), fin_out[:, 64 * d:64 * d + 64]).then_inc(*st.up())

            hin = (view("H", D, 4096) if not prompt else aux(tiles, 0, 1024)).rearrange("p (r g n) -> p r g n", r=2, g=G)
            rows_used = dve_did.now()

            @block.scalar
            def _(act):
                act.wait_ge(*scan_done)
                act.wait_ge(*rows_used)
                nc.scalar.copy(hin[0:64, :, :, 1:n_ch], hs[0:64, :, :, 0:n_ch - 1])
                nc.scalar.copy(hin[64:128, :, :, 0:n_ch - 1], hs[64:128, :, :, n_ch - 2::-1])
                if prompt:
                    nc.scalar.activation(hin[0:64, :, :, 0], h0[0:64], ACT.Copy, scale=0.0)
                    nc.scalar.activation(hin[64:128, :, :, n_ch - 1], h0[64:128], ACT.Copy, scale=0.0).then_inc(*act_did.up())
                else:
                    nc.scalar.copy(hin[0:64, :, :, 0], h0[0:64])
                    nc.scalar.copy(hin[64:128, :, :, n_ch - 1], h0[64:128]).then_inc(*act_did.up())
            hin_ready = act_did.now()
            yield

            t_slot = state["w"] % 2
            toep = wbuf[:, t_slot, :].rearrange("p (g m) -> p g m", g=G)
            state["w"] += 1

            @block.sync
            def _(sp):
                for m in w_last[t_slot]:
                    sp.wait_ge(*m)
                for s in range(S):
                    sp.dma_start(toep[CH * s:CH * s + CH, :, :], kt_dram[:, :, (7 - s) * CH:(7 - s) * CH + P]).then_inc(*w_in[t_slot].up())
            toep_in = w_in[t_slot].now()

            def add_y(i, g):
                @block.vector
                def _(dve):
                    dst = u_c[:, g:g + 4].rearrange("p g s c -> p (g s c)")
                    dve.wait_ge(*filled(i))
                    nc.vector.tensor_tensor(dst, dst, bank(i)[0:n_ch, :], ALU.add).then_inc(*empties(i))
            tap_items = []
            for b in range(8):
                i = take(1)
                w_last[t_slot] = [filled(i)]

                @block.tensor
                def _(pe):
                    if b == 0:
                        pe.wait_ge(*toep_in)
                    open_bank(pe, i)
                    for q in range(4):
                        ins = nc.tensor.matmul(bank(i)[0:n_ch, q * P:(q + 1) * P], xg[:, 4 * b + q, :], toep[:, 4 * b + q, :], start=True, stop=True)
                    ins.then_inc(*fills(i))
                add_y(i, 4 * b)
                tap_items.append(emptied(i))
                yield
            for hf in range(2):
                slot, w, w_mark = load_weights(ca_dram.rearrange("r p (g m) -> p r g m", g=G)[:, :, 16 * hf:16 * hf + 16, :],
                                               lambda a: a.rearrange("p (r g m) -> p r g m", r=2, g=16))
                for b in range(4):
                    i = take(1)
                    w_last[slot] = [filled(i)]

                    @block.tensor
                    def _(pe):
                        if b == 0:
                            pe.wait_ge(*hin_ready)
                            pe.wait_ge(*w_mark)
                        open_bank(pe, i)
                        for q in range(4):
                            g = 4 * b + q
                            for r in range(2):
                                ins = nc.tensor.matmul(bank(i)[0:n_ch, q * P:(q + 1) * P], hin[:, r, 16 * hf + g, :],
                                                       w[:, r, g, :], start=(r == 0), stop=(r == 1))
                        ins.then_inc(*fills(i))

                    @block.vector
                    def _(dve):
                        dve.wait_ge(*tap_items[4 * hf + b])
                    add_y(i, 16 * hf + 4 * b)
                    yield
            y_ready = last_emptied(i)
            g_s = view("TMP", 0, 4096, n_ch).rearrange("p (s c) -> p s c", s=S)

            @block.scalar
            def _(act):
                for m in y_ready:
                    act.wait_ge(*m)
                for s in range(S):
                    ins = nc.scalar.activation(g_s[:, s].rearrange("p (g c) -> p g c", g=G), u_c[:, :, s, :], ACT.Gelu_apprx_tanh)
                ins.then_inc(*act_did.up())
            g_ready = act_did.now()
            yield

            gT = view("Z", 0, 4 * T).rearrange("p (k n s) -> p k n s", k=4, s=S)
            gT_flat = view("Z", 0, 4 * T).rearrange("p (k t) -> p k t", k=4)
            oaT = aux(tiles, 0, 4 * T).rearrange("p (k t) -> p k t", k=4)
            gT_ready = yield from transposes([[g_s[:, s, b * P:(b + 1) * P] for b in range(4)] for s in range(S)],
                                             lambda s: gT[:, :, :, s], [g_ready])
            slot, w, w_mark = load_weights(I["s5_w_glu"][0].rearrange("(k p) n -> p k n", p=P),
                                           lambda a: a[:, 0:2048].rearrange("p (k n) -> p k n", k=4))
            for b in range(4):
                i = take(1)
                w_last[slot] = [filled(i)]

                @block.tensor
                def _(pe):
                    if b == 0:
                        for m in gT_ready:
                            pe.wait_ge(*m)
                        pe.wait_ge(*w_mark)
                    open_bank(pe, i)
                    for k in range(4):
                        ins = nc.tensor.matmul(bank(i)[:, 0:T], w[:, k, b * P:(b + 1) * P], gT_flat[:, k, :], start=(k == 0), stop=(k == 3))
                    ins.then_inc(*fills(i))

                @block.scalar
                def _(act):
                    act.wait_ge(*filled(i))
                    nc.scalar.activation(oaT[:, b, :], bank(i)[:, 0:T], ACT.Sigmoid).then_inc(*empties(i))
                yield
            glu_ready = last_emptied(i)

            @block.vector
            def _(dve):
                for m in glu_ready:
                    dve.wait_ge(*m)
                link(dve, dve_did, nc.vector.tensor_tensor(oaT, oaT, gT_flat, ALU.mult))
            yield
            return oaT, dve_did.now()

        def attention(units, scores, weights, values, keep):
            for n in range(len(units) + 2):
                if n < len(units):
                    scores(n, units[n])
                    yield
                if n > 1:
                    values(n - 2, units[n - 2])
                    yield
                    yield from keep(n - 2, units[n - 2])
                if 0 < n <= len(units):
                    weights(n - 1, units[n - 1])
                    yield

        def mixer0(tiles):
            T = len(tiles) * P
            n_t = len(tiles)
            prompt = tiles == PROMPT
            hT_ready = yield from modulate(0, 0, tiles, I["norm_mix"])
            v_space = view("MOD", 0, n_t * 512).rearrange("p (t n) -> p t n", t=n_t)
            v_project = project(I["even_w_in"][0], 1536, 512, range(n_t), lambda t: v_space[:, t, :], hT_ready)
            pace[0] = 1
            oaT, oa_ready = yield from s5(tiles, hT_ready, v_project)
            yield from v_project
            pace[0] = 4
            z_space = view("Z", 0, n_t * 1536).rearrange("p (t n) -> p t n", t=n_t)
            kctx, sub_row = view("TMP", 1024, 512), view("TMP", 3840, 128)
            vctx, kcT = view("HT", 2048, 512), view("HT", 2560, 512).rearrange("p (b t) -> p b t", b=4)
            ob = view("HT", 3072, 512)
            gain_q, gain_k = view("TMP", 3968, 64), view("TMP", 4032, 64)
            meet()
            ld = group("attention_rows_in")

            @block.sync
            def _(sp):
                sp.dma_start(gain_q, I["diff_q_norm"].to_broadcast([P, DK])).then_inc(*ld.up())
                sp.dma_start(gain_k, I["diff_k_norm"].to_broadcast([P, DK])).then_inc(*ld.up())
                sp.dma_start(sub_row, I["diff_sub_norm"].to_broadcast([P, P])).then_inc(*ld.up())
                sp.dma_start(kctx, I["cache_diff_k"].rearrange("b e t m h d -> (b e t) (m h d)")).then_inc(*ld.up())
            rows_in = ld.now()
            for n in range(2):
                z_ready = yield from project(I["even_w_in"][0], 512 + 512 * n, 512, range(n_t), lambda t, n=n: z_space[:, t, 512 * n:512 * n + 512], hT_ready)
            z_ready = last_emptied(state["items"] - 1)
            ld = group("context_values_in")

            @block.sync
            def _(sp):
                for m in z_ready:
                    sp.wait_ge(*m)
                sp.dma_start(vctx, I["cache_diff_v"].rearrange("b e t h d -> (b e t) (h d)")).then_inc(*ld.up())
            vctx_in = ld.now()
            qk_ready = yield from qk_norm_rope(lambda n: z_space[:, n, :], tiles, [(8, gain_q), (8, gain_k)], view("TMP", 0, 1024), z_ready + [rows_in])
            if prompt:
                st = group("prompt_keys_out")

                @block.sync
                def _(sp):
                    sp.wait_ge(*qk_ready[0])
                    sp.dma_start(O["new_diff_k"].rearrange("b e t m h d -> (b e t) (m h d)"), z_space[:, 0, 512:1024]).then_inc(*st.up())
                    sp.dma_start(O["new_diff_v"].rearrange("b e t h d -> (b e t) (h d)"), v_space[:, 0]).then_inc(*st.up())
            qT = (view("Z", 6144, 2048) if not prompt else view("Z", 2048, 512)).rearrange("p (b t) -> p b t", b=4)
            kT = aux(tiles, 2048, 4 * T).rearrange("p (b t) -> p b t", b=4)
            yield from transposes([[z_space[:, t, b * P:(b + 1) * P] for b in range(4)] for t in range(n_t)],
                                  lambda t: qT[:, :, t * P:(t + 1) * P], qk_ready)
            yield from transposes([[z_space[:, t, 512 + b * P:512 + (b + 1) * P] for b in range(4)] for t in range(n_t)],
                                  lambda t: kT[:, :, t * P:(t + 1) * P], qk_ready)
            T_ready = yield from transposes([[kctx[:, b * P:(b + 1) * P] for b in range(4)]], lambda n: kcT, [rows_in])
            meet("ts")
            pace[0] = 2
            prob = view("TMP", 0, 2560).rearrange("p (s m k) -> p s m k", s=2, m=2)
            aT = view("TMP", 2560, 1280).rearrange("p (s b q) -> p s b q", s=2, b=5)
            obT = view("HT", 0, 4 * T).rearrange("p (k t) -> p k t", k=4)
            nkb = 1 if prompt else 5
            parts = [(0, P, "own")] if prompt else [(0, P, "ctx"), (P, 512, "own")]
            np_ = len(parts)
            first_item = {}

            def scores(u, unit):
                t, hd = unit
                i0 = first_item[u] = take(2 * np_)
                st_ = stat[:, 64 * (u % 2):64 * (u % 2) + 64]

                @block.tensor
                def _(pe):
                    for m in range(2):
                        g = 4 * m + hd
                        rows = slice(64 * (g % 2), 64 * (g % 2) + 64)
                        for n, (k0, kn, what) in enumerate(parts):
                            i = i0 + m * np_ + n
                            open_bank(pe, i)
                            keys = kT[rows, g // 2, :] if what == "own" else kcT[rows, g // 2, :]
                            nc.tensor.matmul(bank(i)[:, 0:kn], qT[rows, g // 2, t * P:(t + 1) * P], keys, start=True, stop=True).then_inc(*fills(i))

                @block.vector
                def _(dve):
                    for m in range(2):
                        for n, (k0, kn, what) in enumerate(parts):
                            i = i0 + m * np_ + n
                            dve.wait_ge(*filled(i))
                            nc.vector.tensor_reduce(st_[:, 2 * m + n:2 * m + n + 1], bank(i)[:, 0:kn], AX, ALU.max).then_inc(*dve_did.up())
                    dve.wait_ge(*dve_did.now())
                    mx = st_[:, 0:4].rearrange("p (m n) -> p m n", n=2)
                    if np_ == 2:
                        link(dve, dve_did, nc.vector.tensor_tensor(mx[:, :, 0], mx[:, :, 0], mx[:, :, 1], ALU.max))
                    link(dve, dve_did, nc.vector.tensor_scalar(st_[:, 4:6], mx[:, :, 0], -SCALE, None, ALU.mult))
                max_ready = dve_did.now()

                @block.scalar
                def _(act):
                    act.wait_ge(*max_ready)
                    for m in range(2):
                        for n, (k0, kn, what) in enumerate(parts):
                            i = i0 + m * np_ + n
                            nc.scalar.activation(prob[:, u % 2, m, k0:k0 + kn], bank(i)[:, 0:kn], ACT.Exp, bias=st_[:, 4 + m:5 + m],
                                                 scale=SCALE, accum_out=st_[:, 8 + 2 * m + n:9 + 2 * m + n]).then_inc(*empties(i))

            after_weights = {}

            def weights(u, unit):
                i0 = first_item[u]
                st_ = stat[:, 64 * (u % 2):64 * (u % 2) + 64]
                w_ = nkb * P
                p0, p1 = prob[:, u % 2, 0, 0:w_], prob[:, u % 2, 1, 0:w_]

                @block.vector
                def _(dve):
                    for n in range(2 * np_):
                        dve.wait_ge(*emptied(i0 + n))
                    z4 = st_[:, 8:12].rearrange("p (m n) -> p m n", n=2)
                    if np_ == 2:
                        link(dve, dve_did, nc.vector.tensor_tensor(st_[:, 6:8], z4[:, :, 0], z4[:, :, 1], ALU.add))
                    else:
                        link(dve, dve_did, nc.vector.tensor_copy(st_[:, 6:8], z4[:, :, 0]))
                    link(dve, dve_did, nc.vector.reciprocal(st_[:, 12:14], st_[:, 6:8]))
                    link(dve, dve_did, nc.vector.scalar_tensor_tensor(st_[:, 14:15], st_[:, 13:14], st_[:, 6:7], neg_lam, ALU.mult, ALU.mult))
                    link(dve, dve_did, nc.vector.scalar_tensor_tensor(p0, p1, st_[:, 14:15], p0, ALU.mult, ALU.add))
                blocks = [prob[:, u % 2, 0, b * P:(b + 1) * P] for b in range(nkb)]
                groups = [blocks[0:4]] + ([blocks[4:5]] if nkb > 4 else [])
                for _ in transposes(groups, lambda n: aT[:, u % 2, 4 * n:min(4 * n + 4, nkb), :], [dve_did.now()]):
                    pass
                after_weights[u] = last_emptied(state["items"] - 1, len(groups))

            def values(u, unit):
                t, hd = unit
                i = take(1)

                @block.tensor
                def _(pe):
                    for m in after_weights[u]:
                        pe.wait_ge(*m)
                    if u == 0:
                        pe.wait_ge(*vctx_in)
                    open_bank(pe, i)
                    own = [v_space[:, b, hd * P:(hd + 1) * P] for b in range(n_t)]
                    vals = own if prompt else [vctx[:, hd * P:(hd + 1) * P]] + own
                    for b in range(nkb):
                        ins = nc.tensor.matmul(bank(i)[:, 0:P], aT[:, u % 2, b, :], vals[b], start=(b == 0), stop=(b == nkb - 1))
                    ins.then_inc(*fills(i))

                @block.vector
                def _(dve):
                    dve.wait_ge(*filled(i))
                    st_ = stat[:, 64 * (u % 2):64 * (u % 2) + 64]
                    nc.vector.tensor_scalar(ob[:, hd * P:(hd + 1) * P], bank(i)[:, 0:P], st_[:, 12:13], None, ALU.mult).then_inc(*empties(i))
                    dve.wait_ge(*emptied(i))

            def keep(u, unit):
                t, hd = unit
                if hd < 3:
                    return
                sqv = view("TMP", 4096, 128)
                o3 = ob.rearrange("p (h d) -> p h d", h=4)
                last = state["items"] - 1

                @block.vector
                def _(dve):
                    dve.wait_ge(*emptied(last))
                    for q in range(4):
                        link(dve, dve_did, nc.vector.tensor_tensor(sqv, o3[:, q], o3[:, q], ALU.mult))
                        link(dve, dve_did, nc.vector.tensor_reduce(stat2[:, q:q + 1], sqv, AX, ALU.add))
                    link(dve, dve_did, nc.vector.tensor_scalar(stat2[:, 0:4], stat2[:, 0:4], 1.0 / P, EPS, ALU.mult, ALU.add))
                var_ready = dve_did.now()

                @block.scalar
                def _(act):
                    act.wait_ge(*var_ready)
                    nc.scalar.activation(stat2[:, 16:20], stat2[:, 0:4], ACT.Sqrt).then_inc(*act_did.up())
                std_ready = act_did.now()

                @block.vector
                def _(dve):
                    dve.wait_ge(*std_ready)
                    link(dve, dve_did, nc.vector.reciprocal(stat2[:, 20:24], stat2[:, 16:20]))
                    link(dve, dve_did, nc.vector.tensor_scalar(stat2[:, 20:24], stat2[:, 20:24], 1.0 - LAM_INIT, None, ALU.mult))
                    link(dve, dve_did, nc.vector.tensor_tensor(o3, o3, stat2[:, 20:24].unsqueeze(2).to_broadcast([P, 4, P]), ALU.mult))
                    link(dve, dve_did, nc.vector.tensor_tensor(o3, o3, sub_row.unsqueeze(1).to_broadcast([P, 4, P]), ALU.mult))
                done = yield from transposes([[ob[:, b * P:(b + 1) * P] for b in range(4)]], lambda n: obT[:, :, t * P:(t + 1) * P], [dve_did.now()])

                @block.vector
                def _(dve):
                    dve.wait_ge(*done[-1])

            yield from attention([(t, hd) for t in range(n_t) for hd in range(4)], scores, weights, values, keep)
            meet()
            yield from out_project(I["even_w_out"][0], tiles, lambda k: oaT[:, k, :] if k < 4 else obT[:, k - 4, :], [oa_ready])

        def mixer1(tiles, parts):
            T = len(tiles) * P
            n_t = len(tiles)
            prompt = tiles == PROMPT
            hT_ready = yield from modulate(1, 0, tiles, I["norm_mix"], parts[0])
            zo = view("Z", 0, n_t * ODD_IN).rearrange("p (t n) -> p t n", t=n_t)
            pool_m = view("TMP", 0, 3072).rearrange("p (m w s) -> p m w s", m=6, w=4)
            plT = view("TMP", 3072, 512)
            gain_q, gain_k = view("TMP", 4352, 64), view("TMP", 4416, 64)
            pw_sb = aux(tiles, 2304, 512).rearrange("p (w d) -> p w d", w=4)
            kc1, vc1 = view("TMP", 4096, 128), view("TMP", 4224, 128)
            meet()
            ld = group("odd_rows_in")

            @block.sync
            def _(sp):
                sp.dma_start(pool_m.rearrange("p m w s -> p (m w s)"), I["pool_bands"]).then_inc(*ld.up())
                sp.dma_start(gain_q, I["win_q_norm"].to_broadcast([P, DK])).then_inc(*ld.up())
                sp.dma_start(gain_k, I["win_k_norm"].to_broadcast([P, DK])).then_inc(*ld.up())
                sp.dma_start(kc1, I["cache_win_k"].rearrange("b e t h d -> (b e t) (h d)")).then_inc(*ld.up())
                sp.dma_start(vc1, I["cache_win_v"].rearrange("b e t h d -> (b e t) (h d)")).then_inc(*ld.up())
                sp.dma_start(sink_col, I["win_sink"].to_broadcast([P, 8])).then_inc(*ld.up())
                sp.dma_start(pw_sb, I["pool_w"][0].rearrange("w c d -> c w d")).then_inc(*ld.up())
                with nc.allow_non_contiguous_dma(reason="a short column vector"):
                    sp.dma_start(pscale_col, I["pool_scale"].rearrange("a (w d) -> d (a w)", w=4)).then_inc(*ld.up())
            rows_in = ld.now()
            z_all, qk_ready = [], []
            pace[0] = 4
            for part in parts:
                if part != parts[0]:
                    while tiles_summed[0] < NT:
                        yield
                    hT_ready = yield from modulate(1, 0, tiles, I["norm_mix"], part)
                places = [t - tiles[0] for t in part]
                for col0, n in ((0, 512), (512, 256), (768, 512)):
                    yield from project(I["odd_w_in"][0], col0, n, places, lambda t, col0=col0, n=n: zo[:, t, col0:col0 + n], hT_ready)
                z_ready = last_emptied(state["items"] - 1)
                z_all += z_ready
                meet("v")
                qk_ready = yield from qk_norm_rope(lambda n: zo[:, places[n], :], part, [(8, gain_q), (2, gain_k)], aux(tiles, 0, 640), z_ready + [rows_in])
            meet("s")
            ocT = view("HT", 0, 4 * T).rearrange("p (k t) -> p k t", k=4)
            odT = view("HT", 2048, 4 * T).rearrange("p (k t) -> p k t", k=4)
            for wd in range(4):
                i = take(1)

                @block.tensor
                def _(pe):
                    if wd == 0:
                        for m in z_all + [rows_in]:
                            pe.wait_ge(*m)
                    open_bank(pe, i)
                    for t in range(n_t):
                        srcs = [(t, 0 if prompt else 1 if t == 0 else 3 if t == n_t - 1 else 2)]
                        if t:
                            srcs.append((t - 1, 4))
                        if t < n_t - 1:
                            srcs.append((t + 1, 5))
                        for n, (tt, m) in enumerate(srcs):
                            ins = nc.tensor.matmul(bank(i)[:, t * P:(t + 1) * P], zo[:, tt, 768 + wd * P:768 + (wd + 1) * P], pool_m[:, m, wd, :],
                                                   start=(n == 0), stop=(n == len(srcs) - 1))
                    ins.then_inc(*fills(i))

                @block.scalar
                def _(act):
                    if wd:
                        act.wait_ge(*emptied(i - 1))
                    act.wait_ge(*filled(i))
                    nc.scalar.copy(plT[:, 0:T], bank(i)[:, 0:T]).then_inc(*empties(i))
                i1 = take(1)

                @block.tensor
                def _(pe):
                    pe.wait_ge(*emptied(i))
                    open_bank(pe, i1)
                    nc.tensor.matmul(bank(i1)[:, 0:T], pw_sb[:, wd, :], plT[:, 0:T], start=True, stop=True).then_inc(*fills(i1))

                @block.scalar
                def _(act):
                    act.wait_ge(*filled(i1))
                    nc.scalar.activation(odT[:, wd, :], bank(i1)[:, 0:T], ACT.Copy, scale=pscale_col[:, wd:wd + 1]).then_inc(*empties(i1))
                yield
            meet("v")
            if prompt:
                st = group("prompt_keys_out")

                @block.sync
                def _(sp):
                    sp.wait_ge(*qk_ready[0])
                    sp.dma_start(O["new_win_k"].rearrange("b e t h d -> (b e t) (h d)"), zo[:, 0, 512:640]).then_inc(*st.up())
                    sp.dma_start(O["new_win_v"].rearrange("b e t h d -> (b e t) (h d)"), zo[:, 0, 640:768]).then_inc(*st.up())
            n_k = n_t + 1
            kdup = view("TMP", 1024, n_k * 256).rearrange("p (t n r d) -> p t n r d", t=n_k, n=2, r=2)

            @block.vector
            def _(dve):
                for r in range(2):
                    for t in range(n_t):
                        nc.vector.tensor_copy(kdup[:, t, :, r, :], zo[:, t, 512:640].rearrange("p (n d) -> p n d", n=2)).then_inc(*dve_did.up())
                    nc.vector.tensor_copy(kdup[:, n_t, :, r, :], kc1.rearrange("p (n d) -> p n d", n=2)).then_inc(*dve_did.up())
            dup_ready = dve_did.now()
            qT = (view("Z", 5120, 2048) if not prompt else view("Z", 2048, 512)).rearrange("p (b t) -> p b t", b=4)
            yield from transposes([[zo[:, t, b * P:(b + 1) * P] for b in range(4)] for t in range(n_t)],
                                  lambda t: qT[:, :, t * P:(t + 1) * P], qk_ready)
            kT = aux(tiles, 0, 2 * n_k * P).rearrange("p (n t) -> p n t", n=2)
            yield from transposes([[kdup[:, t, n].rearrange("p r d -> p (r d)") for n in range(2)] for t in range(n_k)],
                                  lambda t: kT[:, :, t * P:(t + 1) * P], [dup_ready])
            meet("tsv")
            pace[0] = 2
            oc = aux(tiles, 1536, 512)
            prob = view("TMP", 0, 2048).rearrange("p (s e k) -> p s e k", s=2, e=2)
            aT = view("TMP", 2048, 2048).rearrange("p (s e b q) -> p s e b q", s=2, e=2, b=4)
            first_item, after_weights = {}, {}

            def shape(t):
                if prompt:
                    return [(0, 0, P)], 1, [], [zo[:, 0, 640:768]]
                lo, hi = max(t - 1, 0), min(t + 1, n_t - 1)
                nkb = hi - lo + 2
                masks = ([1] if t else []) + ([nkb - 1] if t < n_t - 1 else [])
                return ([(0, n_t * P, P), (P, lo * P, (nkb - 1) * P)], nkb, masks,
                        [vc1] + [zo[:, b, 640:768] for b in range(lo, hi + 1)])

            def scores(u, unit):
                t, pair = unit
                segs, nkb, masks, vals = shape(t)
                st_ = stat[:, 64 * (u % 2):64 * (u % 2) + 64]
                i0 = first_item[u] = take(2)
                sink = sink_col[:, 2 * pair:2 * pair + 2]

                @block.tensor
                def _(pe):
                    for e in range(2):
                        rows = slice(64 * e, 64 * e + 64)
                        open_bank(pe, i0 + e)
                        for (o, k0, kn) in segs:
                            ins = nc.tensor.matmul(bank(i0 + e)[:, o:o + kn], qT[rows, pair, t * P:(t + 1) * P], kT[rows, pair // 2, k0:k0 + kn],
                                                   start=True, stop=True)
                        ins.then_inc(*fills(i0 + e))

                @block.vector
                def _(dve):
                    for e in range(2):
                        dve.wait_ge(*filled(i0 + e))
                        blocks = bank(i0 + e).rearrange("p (b k) -> p b k", k=P)
                        if len(masks) == 2:
                            edges = bank(i0 + e).rearrange("p (c b k) -> p c b k", b=2, k=P)[:, :, 1, :]
                            link(dve, dve_did, nc.vector.tensor_tensor(edges, edges, mask_both, ALU.add))
                        for b in masks if len(masks) == 1 else []:
                            link(dve, dve_did, nc.vector.tensor_tensor(blocks[:, b], blocks[:, b], mask_before if t else mask_after, ALU.add))
                        nc.vector.tensor_reduce(st_[:, e:e + 1], bank(i0 + e)[:, 0:nkb * P], AX, ALU.max).then_inc(*dve_did.up())
                    dve.wait_ge(*dve_did.now())
                    link(dve, dve_did, nc.vector.scalar_tensor_tensor(st_[:, 2:4], st_[:, 0:2], SCALE, sink, ALU.mult, ALU.max))
                    link(dve, dve_did, nc.vector.tensor_scalar(st_[:, 4:6], st_[:, 2:4], -1.0, None, ALU.mult))
                    nc.vector.tensor_tensor(st_[:, 8:10], st_[:, 4:6], sink, ALU.add).then_inc(*dve_did.up())
                max_ready = dve_did.now()

                @block.scalar
                def _(act):
                    act.wait_ge(*max_ready)
                    nc.scalar.activation(st_[:, 10:12], st_[:, 8:10], ACT.Exp)
                    for e in range(2):
                        nc.scalar.activation(prob[:, u % 2, e, 0:nkb * P], bank(i0 + e)[:, 0:nkb * P], ACT.Exp, bias=st_[:, 4 + e:5 + e],
                                             scale=SCALE, accum_out=st_[:, 6 + e:7 + e]).then_inc(*empties(i0 + e))

            def weights(u, unit):
                nkb = shape(unit[0])[1]
                st_ = stat[:, 64 * (u % 2):64 * (u % 2) + 64]
                exps = [emptied(first_item[u] + e) for e in range(2)]
                for _ in transposes([[prob[:, u % 2, e, b * P:(b + 1) * P] for b in range(nkb)] for e in range(2)],
                                    lambda e: aT[:, u % 2, e, 0:nkb, :], exps):
                    pass
                after_weights[u] = last_emptied(state["items"] - 1, 2)

                @block.vector
                def _(dve):
                    for m in exps:
                        dve.wait_ge(*m)
                    link(dve, dve_did, nc.vector.tensor_tensor(st_[:, 12:14], st_[:, 6:8], st_[:, 10:12], ALU.add))
                    link(dve, dve_did, nc.vector.reciprocal(st_[:, 14:16], st_[:, 12:14]))

            def values(u, unit):
                t, pair = unit
                nkb, vals = shape(t)[1], shape(t)[3]
                kv = pair // 2
                st_ = stat[:, 64 * (u % 2):64 * (u % 2) + 64]
                i = take(1)

                @block.tensor
                def _(pe):
                    for m in after_weights[u]:
                        pe.wait_ge(*m)
                    open_bank(pe, i)
                    for e in range(2):
                        for b in range(nkb):
                            ins = nc.tensor.matmul(bank(i)[:, e * DK:(e + 1) * DK], aT[:, u % 2, e, b, :], vals[b][:, kv * DK:(kv + 1) * DK],
                                                   start=(b == 0), stop=(b == nkb - 1))
                    ins.then_inc(*fills(i))

                @block.vector
                def _(dve):
                    dve.wait_ge(*filled(i))
                    nc.vector.tensor_tensor(oc[:, pair * P:(pair + 1) * P].rearrange("p (e d) -> p e d", e=2),
                                            bank(i)[:, 0:P].rearrange("p (e d) -> p e d", e=2),
                                            st_[:, 14:16].unsqueeze(2).to_broadcast([P, 2, DK]), ALU.mult).then_inc(*empties(i))
                    dve.wait_ge(*emptied(i))

            def keep(u, unit):
                t, pair = unit
                if pair < 3:
                    return
                last = emptied(state["items"] - 1)
                done = yield from transposes([[oc[:, b * P:(b + 1) * P] for b in range(4)]], lambda n: ocT[:, :, t * P:(t + 1) * P], [last])

                @block.vector
                def _(dve):
                    dve.wait_ge(*done[-1])

            yield from attention([(t, pair) for t in range(n_t) for pair in range(4)], scores, weights, values, keep)
            meet()
            yield from out_project(I["odd_w_out"][0], tiles, lambda k: ocT[:, k, :] if k < 4 else odT[:, k - 4, :], [])

        slot_in = [sem(f"expert_row_in{j}") for j in range(RING)]
        u_used, v_used, diag_ready = sem("u_rows_used"), sem("v_rows_used"), sem("diagonals_ready")
        staged, w_staged, granted = sem("indices_staged"), sem("weights_staged"), sem("slots_granted")
        acc_used, w_granted = sem("v_rows_added"), sem("weights_space_granted")
        dots_kept, sum_done, sum_read = count("dots_kept"), count("expert_sum_done"), count("expert_sum_read")
        ring = view("RING", 0, RING * D).rearrange("p (j d) -> p j d", j=RING)
        expert = view("PEER", 0, 640).bitcast(U32).rearrange("p (t n) -> p t n", t=NT)
        gate = view("PEER", 640, 640).rearrange("p (t n) -> p t n", t=NT)
        dots = view("PEER", 1280, 128)
        w_all = view("PEER", 1408, 128)
        diag = view("PEER", 1536, DIAGS * P).rearrange("p (s n) -> p s n", s=DIAGS)
        aslot = view("PEER", 2176, 2 * RING)
        islot = view("PEER", 2208, 2 * RING).bitcast(U32).rearrange("p (s n) -> p s n", s=2)
        wslot = view("PEER", 2240, 2 * RING).rearrange("p (s n) -> p s n", s=2)
        peer_rounds, peer_tiles, tiles_summed = [0], [0], [0]

        @block.tensor
        def _(pe):
            pe.sem_inc(v_used, DIAGS)

        def top16(dve, lists):
            v = nc.vector
            for step in (lambda src, out, idx: v.max(out[:, 0:8], src),
                         lambda src, out, idx: v.max_index(idx[:, 0:8], out[:, 0:8], src),
                         lambda src, out, idx: v.match_replace(src, out[:, 0:8], src, -3.0e38),
                         lambda src, out, idx: v.max(out[:, 8:16], src),
                         lambda src, out, idx: v.max_index(idx[:, 8:16], out[:, 8:16], src)):
                for src, out, idx in lists:
                    step(src, out, idx).then_inc(*dve_did.up())
                dve.wait_ge(*dve_did.now())

        vals1 = view("MOD", 0, 256).rearrange("p (c k) -> p c k", c=16)
        idx1 = view("MOD", 256, 256).bitcast(U32).rearrange("p (c k) -> p c k", c=16)

        def route_scores(l, tiles, ready):
            T, n_t = len(tiles) * P, len(tiles)
            s_all = view("Z", 0, n_t * 2048).rearrange("p (t n) -> p t n", t=n_t)
            sub_k = view("TMP", 0, 2048).rearrange("p (c k) -> p c k", c=16)
            qpT = view("TMP", 2048, 4 * T).rearrange("p (c t) -> p c t", c=4)
            meet("ys")
            ld = group("sub_keys_in")

            @block.sync
            def _(sp):
                sp.dma_start(sub_k, I["peer_sub_keys"][l]).then_inc(*ld.up())
            keys_in = ld.now()
            before = []

            def first_tile_list(c, scored):
                @block.vector
                def _(dve):
                    dve.wait_ge(*scored)
                    top16(dve, [(s_all[:, 0, b * P:(b + 1) * P], vals1[:, b], idx1[:, b]) for b in (c, c + 1)])
            for blk in range(4):
                slot, w, w_mark = load_weights(I["peer_w_q"][l].rearrange("(k p) n -> p k n", p=P)[:, :, blk * 512:(blk + 1) * 512],
                                               lambda a: a.rearrange("p (k n) -> p k n", k=KD))
                for c in range(4):
                    i = take(1)
                    w_last[slot] = [filled(i)]

                    @block.tensor
                    def _(pe):
                        if blk == 0 and c == 0:
                            for m in ready:
                                pe.wait_ge(*m)
                            pe.wait_ge(*keys_in)
                        if c == 0:
                            pe.wait_ge(*w_mark)
                        open_bank(pe, i)
                        for k in range(KD):
                            ins = nc.tensor.matmul(bank(i)[:, 0:T], w[:, k, c * P:(c + 1) * P], hT[:, k, 0:T], start=(k == 0), stop=(k == KD - 1))
                        ins.then_inc(*fills(i))

                    @block.scalar
                    def _(act):
                        for m in before:
                            act.wait_ge(*m)
                        act.wait_ge(*filled(i))
                        nc.scalar.copy(qpT[:, c, :], bank(i)[:, 0:T]).then_inc(*empties(i))
                    before = []
                    if blk and c % 2 == 0:
                        first_tile_list(4 * blk - 4 + c, scored)
                    yield
                q_ready = last_emptied(i, 4)
                for n in range(n_t):
                    i = take(1)

                    @block.tensor
                    def _(pe):
                        for m in q_ready:
                            pe.wait_ge(*m)
                        open_bank(pe, i)
                        for c in range(4):
                            ins = nc.tensor.matmul(bank(i)[:, c * P:(c + 1) * P], qpT[:, c, n * P:(n + 1) * P], sub_k[:, 4 * blk + c, :],
                                                   start=True, stop=True)
                        ins.then_inc(*fills(i))

                    @block.scalar
                    def _(act):
                        act.wait_ge(*filled(i))
                        nc.scalar.copy(s_all[:, n, blk * 512:(blk + 1) * 512], bank(i)).then_inc(*empties(i))
                    q_ready = []
                    before = last_emptied(i, 1)
                    if n == 0:
                        scored = emptied(i)
                    if n % 2:
                        yield
            for c in (12, 14):
                first_tile_list(c, scored)
                yield

        routed = {}

        def route(l, t, n, n_t):
            s_all = view("Z", 0, n_t * 2048).rearrange("p (t n) -> p t n", t=n_t)

            def tmp(start, size):
                return view("TMP", start, size)
            idx1f = tmp(512, 256).rearrange("p (c k) -> p c k", c=16)
            cand = [tmp(768, 256), tmp(4096, 256)]
            best = tmp(1024, 128).rearrange("p (h k) -> p h k", h=HEADS)
            pos, posj = tmp(1152, 128).bitcast(U32), tmp(3840, 128).bitcast(U32)
            j1f, j2f, e1f, e2f = tmp(1280, 128), tmp(1408, 128), tmp(1536, 128), tmp(1664, 128)
            sel = tmp(1792, 2048)
            esum = tmp(3968, 16)
            for c in range(0, 16 if n else 0, 2):
                @block.vector
                def _(dve):
                    top16(dve, [(s_all[:, n, b * P:(b + 1) * P], vals1[:, b], idx1[:, b]) for b in (c, c + 1)])
                yield
            pos3 = pos.rearrange("p (h k) -> p h k", h=HEADS)
            for hd in range(0, HEADS, 2):
                @block.vector
                def _(dve):
                    for e in range(2):
                        nc.vector.tensor_tensor(
                            cand[e].rearrange("p (a b) -> p a b", a=TOPK), vals1[:, 2 * (hd + e)].unsqueeze(2).to_broadcast([P, TOPK, TOPK]),
                            vals1[:, 2 * (hd + e) + 1].unsqueeze(1).to_broadcast([P, TOPK, TOPK]), ALU.add).then_inc(*dve_did.up())
                    dve.wait_ge(*dve_did.now())
                    top16(dve, [(cand[e], best[:, hd + e], pos3[:, hd + e]) for e in range(2)])
                yield

            @block.vector
            def _(dve):
                v = nc.vector
                link(dve, dve_did, v.tensor_copy(idx1f, idx1))
                link(dve, dve_did, v.tensor_scalar(posj, pos, 4, None, ALU.logical_shift_right))
                link(dve, dve_did, v.tensor_copy(j1f, posj))
                link(dve, dve_did, v.tensor_scalar(posj, pos, 15, None, ALU.bitwise_and))
                link(dve, dve_did, v.tensor_copy(j2f, posj))
            sel3 = sel.rearrange("p (n j) -> p n j", j=TOPK)
            sel4 = sel.rearrange("p (h k j) -> p h k j", h=HEADS, k=TOPK)
            idx4 = idx1f.rearrange("p (h c) k -> p h c k", c=2)
            for half, (jf, ef) in enumerate(((j1f, e1f), (j2f, e2f))):
                @block.vector
                def _(dve):
                    v = nc.vector
                    link(dve, dve_did, v.tensor_tensor(sel3, jf.unsqueeze(2).to_broadcast([P, HK, TOPK]),
                                                       iota16.unsqueeze(1).to_broadcast([P, HK, TOPK]), ALU.is_equal))
                    link(dve, dve_did, v.tensor_tensor(sel4, sel4, idx4[:, :, half].unsqueeze(2).to_broadcast([P, HEADS, TOPK, TOPK]), ALU.mult))
                    link(dve, dve_did, v.tensor_reduce(ef, sel3, AX, ALU.add))
                yield
            g3 = gate[:, t].rearrange("p (h k) -> p h k", h=HEADS)

            @block.vector
            def _(dve):
                v = nc.vector
                if l:
                    dve.wait_ge(staged, (t + 1) * 2 * ROUNDS)
                link(dve, dve_did, v.tensor_scalar(e1f, e1f, 128.0, float(l * EXPERTS), ALU.mult, ALU.add))
                link(dve, dve_did, v.tensor_tensor(e1f, e1f, e2f, ALU.add))
                link(dve, dve_did, v.tensor_copy(expert[:, t], e1f))
                link(dve, dve_did, v.tensor_tensor(g3, best, best[:, :, 0:1].to_broadcast([P, HEADS, TOPK]), ALU.subtract))
            shifted = dve_did.now()

            @block.scalar
            def _(act):
                act.wait_ge(*shifted)
                nc.scalar.activation(gate[:, t], gate[:, t], ACT.Exp).then_inc(*act_did.up())
            exped = act_did.now()

            @block.vector
            def _(dve):
                v = nc.vector
                dve.wait_ge(*exped)
                link(dve, dve_did, v.tensor_reduce(esum[:, 0:8], g3, AX, ALU.add))
                link(dve, dve_did, v.reciprocal(esum[:, 8:16], esum[:, 0:8]))
                link(dve, dve_did, v.tensor_tensor(g3, g3, esum[:, 8:16].unsqueeze(2).to_broadcast([P, HEADS, TOPK]), ALU.mult))
            routed[l, t] = dve_did.now()
            yield

        def prepare_experts(l, tiles):
            ready = yield from modulate(l, 1, tiles, I["norm_ffn"])
            yield from route_scores(l, tiles, ready)
            meet("v")

        def u_free(pool, j, r):
            pool.wait_ge(u_used, r * RING + (j + 1))

        def v_free(pool, j, r):
            if j in PE_ROWS:
                pool.wait_ge(v_used, r * len(PE_ROWS) + (DIAGS + PE_ROWS.index(j) + 1))
            else:
                pool.wait_ge(acc_used, r * len(DVE_ROWS) + (DVE_ROWS.index(j) + 1))

        def gather_rounds(table, t, first, first_round, later, later_round, ready):
            s0 = peer_rounds[0]
            peer_rounds[0] += ROUNDS

            def one_round(pool, r, parity, wait_of):
                nc.gpsimd.tensor_copy(islot[:, parity], expert[:, t, bass.ds(r * RING, RING)]).then_inc(staged, 1)
                for j in range(RING):
                    if j == 0:
                        pool.wait_ge(staged, r + (s0 + 1))
                        pool.sem_inc(granted, 1)
                    wait_of(j)
                    pool.sem_inc(granted, 1)
                    nc.gpsimd.indirect_dma_start(out=ring[:, j, :], out_offset=None, in_=table,
                                                 in_offset=bass.IndirectOffsetOnAxis(ap=islot[:, parity, j:j + 1], axis=0)
                                                 ).then_inc(slot_in[j], 16)

            @block.gpsimd
            def _(pool):
                pool.wait_ge(*ready)

                def first_wait(j):
                    if first is not None:
                        first(pool, j, first_round)
                one_round(pool, 0, 0, first_wait)
                one_round(pool, 1, 1, lambda j: later(pool, j, later_round))
                with pool.Fori(1, ROUNDS // 2) as i:
                    for parity in range(2):
                        one_round(pool, i * 2 + parity, parity,
                                  lambda j, parity=parity: later(pool, j, i * 2 + (parity - 1 + later_round)))
            return s0

        tables = [I["peer_u"].rearrange("l e d -> (l e) d"), I["peer_v"].rearrange("l e d -> (l e) d")]
        PAIR = 2 * RING
        NP, ND = len(PE_ROWS), len(DVE_ROWS)

        def experts(l, t, beside, u_every, v_every):
            while (l, t) not in routed:
                next(beside)
            k = peer_tiles[0]
            peer_tiles[0] += 1
            s_u = gather_rounds(tables[0], t, v_free if k else None, ROUNDS * k - 1, u_free, ROUNDS * k, routed[l, t])
            s_v = gather_rounds(tables[1], t, u_free, ROUNDS * (k + 1) - 1, v_free, ROUNDS * k, routed[l, t])
            alone = object()
            done = False

            def piece():
                nonlocal done
                if not done and next(beside, alone) is alone:
                    done = True

            def dot(dve, j, arrival, kept):
                dve.wait_ge(slot_in[j], arrival)
                nc.vector.tensor_tensor_reduce(ring[:, j, :], ring[:, j, :], h[:, t, :], 1.0, 0.0, ALU.mult, ALU.add,
                                               kept).then_inc(u_used, 1)
            n = 0
            while n < HK and not done:
                if n % RING == 0:
                    u_step = u_every()

                @block.vector
                def _(dve):
                    for m in range(n, n + u_step):
                        dot(dve, m % RING, 16 * (s_u + m // RING + 1), dots[:, m:m + 1])
                n += u_step
                piece()
            if n < HK:
                full_pair = -(-n // PAIR)

                @block.vector
                def _(dve):
                    for m in range(n, full_pair * PAIR):
                        dot(dve, m % RING, 16 * (s_u + m // RING + 1), dots[:, m:m + 1])
                    if full_pair * PAIR < HK:
                        with dve.Fori(full_pair, HK // PAIR) as i:
                            for m in range(PAIR):
                                dot(dve, m % RING, i * 32 + 16 * (s_u + m // RING + 1), aslot[:, m:m + 1])
                            dve.wait_ge(u_used, i * PAIR + (HK * k + PAIR))
                            dve.wait_ge(dots_kept.sem, (i - full_pair) + dots_kept.n) if dots_kept.n else None
                            nc.vector.tensor_copy(dots[:, bass.ds(i * PAIR, PAIR)], aslot).then_inc(dots_kept.sem, 1)
                            dve.wait_ge(dots_kept.sem, (i - full_pair) + (dots_kept.n + 1))
                        dots_kept.n += HK // PAIR - full_pair

            @block.scalar
            def _(act):
                act.wait_ge(u_used, HK * (k + 1))
                if dots_kept.n:
                    act.wait_ge(*dots_kept.now())
                nc.scalar.activation(dots, dots, ACT.Gelu_apprx_tanh).then_inc(*act_did.up())
            gelued = act_did.now()
            acc = h[:, t]

            @block.vector
            def _(dve):
                dve.wait_ge(*gelued)
                if k:
                    dve.wait_ge(w_staged, ROUNDS * k)
                nc.vector.tensor_tensor(w_all, dots, gate[:, t], ALU.mult).then_inc(*dve_did.up())
            weighted = dve_did.now()

            @block.vector
            def _(dve):
                link(dve, dve_did, nc.vector.memset(acc, 0.0))

            def stage_weights(act, r, parity):
                if not isinstance(r, int) or ROUNDS * k + r > 1:
                    act.wait_ge(acc_used, r * ND + ND * (ROUNDS * k - 1))
                act.sem_inc(w_granted, 1)
                nc.scalar.copy(wslot[:, parity], w_all[:, bass.ds(r * RING, RING)]).then_inc(w_staged, 1)
                act.wait_ge(w_staged, r + (ROUNDS * k + 1))

            def v_round(act, pe, dve, r, parity, rows):
                if act is not None:
                    if rows[0] == 0:
                        stage_weights(act, r, parity)
                    for j in rows:
                        if j in PE_ROWS:
                            q = PE_ROWS.index(j)
                            act.wait_ge(v_used, r * NP + (NP * ROUNDS * k + q + 1))
                            nc.scalar.activation(diag[:, q % DIAGS], ident, ACT.Copy, scale=wslot[:, parity, j:j + 1]).then_inc(diag_ready, 1)
                if pe is not None:
                    for j in rows:
                        if j in PE_ROWS:
                            q = PE_ROWS.index(j)
                            pe.wait_ge(slot_in[j], r * 16 + (16 * s_v + 16))
                            pe.wait_ge(diag_ready, r * NP + (NP * ROUNDS * k + q + 1))
                            nc.tensor.matmul(ps[:, BANKS], diag[:, q % DIAGS], ring[:, j, 0:512], start=False, stop=False)
                            nc.tensor.matmul(ps[:, BANKS + 1], diag[:, q % DIAGS], ring[:, j, 512:1024], start=False, stop=False).then_inc(v_used, 1)
                if dve is not None:
                    for j in rows:
                        if j in DVE_ROWS:
                            q = DVE_ROWS.index(j)
                            dve.wait_ge(slot_in[j], r * 16 + (16 * s_v + 16))
                            if q == 0:
                                dve.wait_ge(w_staged, r + (ROUNDS * k + 1))
                            if not isinstance(r, int) or ND * (ROUNDS * k + r) + q:
                                dve.wait_ge(acc_used, r * ND + (ND * ROUNDS * k + q))
                            nc.vector.scalar_tensor_tensor(acc, ring[:, j, :], wslot[:, parity, j:j + 1], acc, ALU.mult, ALU.add).then_inc(acc_used, 1)

            @block.scalar
            def _(act):
                act.wait_ge(*weighted)
            zeros = zero_w[:, 0:1].to_broadcast([P, 512])

            @block.tensor
            def _(pe):
                if k:
                    pe.wait_ge(*sum_read.now())
                for b in range(2):
                    nc.tensor.matmul(ps[:, BANKS + b], zero_w, zeros, start=True, stop=False)
            n, step = 0, RING
            while n < HK and not done:
                if n % RING == 0:
                    step = v_every()
                rows = range(n % RING, n % RING + step)

                @block.scalar
                def _(act):
                    v_round(act, None, None, n // RING, n // RING % 2, rows)
                piece()

                @block.tensor
                def _(pe):
                    v_round(None, pe, None, n // RING, n // RING % 2, rows)

                @block.vector
                def _(dve):
                    v_round(None, None, dve, n // RING, n // RING % 2, rows)
                n += step
            if n < HK:
                full_pair = -(-n // PAIR)

                def rest(act, pe, dve, eng):
                    for m in range(n, full_pair * PAIR, step):
                        v_round(act, pe, dve, m // RING, m // RING % 2, range(m % RING, m % RING + step))
                    if full_pair * PAIR < HK:
                        with eng.Fori(full_pair, HK // PAIR) as i:
                            for parity in range(2):
                                v_round(act, pe, dve, i * 2 + parity, parity, range(RING))

                @block.scalar
                def _(act):
                    rest(act, None, None, act)

                @block.tensor
                def _(pe):
                    rest(None, pe, None, pe)

                @block.vector
                def _(dve):
                    rest(None, None, dve, dve)

            @block.tensor
            def _(pe):
                for b in range(2):
                    nc.tensor.matmul(ps[:, BANKS + b], zero_w, zeros, start=False, stop=True).then_inc(*sum_done.up())
            in_banks = sum_done.now()
            piece()

            @block.vector
            def _(dve):
                dve.wait_ge(*in_banks)
                dve.wait_ge(acc_used, ND * ROUNDS * (k + 1))
                for half in range(2):
                    cols = slice(half * 512, (half + 1) * 512)
                    nc.vector.tensor_tensor(acc[:, cols], ps[:, BANKS + half], acc[:, cols], ALU.add).then_inc(*sum_read.up())
                dve.wait_ge(*sum_read.now())
                link(dve, dve_did, nc.vector.tensor_tensor(acc, acc, gates[:, min(t, 1)], ALU.mult))
                link(dve, dve_did, nc.vector.tensor_tensor(x[:, t], x[:, t], acc, ALU.add))
            tiles_summed[0] += 1

        def prompt0():
            yield from mixer0(PROMPT)
            yield from prepare_experts(0, PROMPT)
            yield from route(0, 0, 0, 1)

        def sample0():
            yield from mixer0(SAMPLE)
            yield from prepare_experts(0, SAMPLE)
            for n, t in enumerate(SAMPLE):
                yield from route(0, t, n, 4)

        def prompt1():
            for which in range(2):
                yield from ada(1, which)
            yield from mixer1(PROMPT, [PROMPT])
            yield from prepare_experts(1, PROMPT)
            yield from route(1, 0, 0, 1)

        def sample1():
            while tiles_summed[0] < NT - 1:
                yield
            yield from mixer1(SAMPLE, [SAMPLE[:-1], SAMPLE[-1:]])
            yield from prepare_experts(1, SAMPLE)
            for n, t in enumerate(SAMPLE):
                yield from route(1, t, n, 4)

        def then(*gens):
            for g in gens:
                yield from g
        for _ in prompt0():
            pass
        beside = then(sample0(), prompt1(), sample1())
        experts(0, 0, beside, lambda: pace[0], lambda: 2)
        for t in SAMPLE:
            experts(0, t, beside, lambda: 4 if (0, SAMPLE[-1]) in routed else 8, lambda: 4)
        while (1, 0) not in routed:
            next(beside)
        experts(1, 0, beside, lambda: pace[0], lambda: 2)
        st = group("prompt_out")

        @block.sync
        def _(sp):
            sp.wait_ge(*dve_did.now())
            sp.dma_start(O["y_prompt"][0], x[:, 0, :]).then_inc(*st.up())
        while (1, 4) not in routed and (1, 1) not in routed:
            next(beside)
        for t in SAMPLE:
            experts(1, t, beside, lambda: HK, lambda: RING)
        st2 = group("sample_out")

        @block.sync
        def _(sp):
            sp.wait_ge(*dve_did.now())
            sp.dma_start(O["y_sample"][0].rearrange("(t p) d -> p t d", p=P), x[:, 1:5, :]).then_inc(*st2.up())
            sp.wait_ge(*st.now())
            sp.wait_ge(*st2.now())


_OUTS = [("y_prompt", (1, 128, 1024)), ("y_sample", (1, 512, 1024)), ("new_diff_k", (1, 1, 128, 2, 4, 64)),
         ("new_diff_v", (1, 1, 128, 4, 128)), ("new_s5", (1, 1, 2, 2, 32, 64)), ("new_win_k", (1, 1, 128, 2, 64)),
         ("new_win_v", (1, 1, 128, 2, 64))]
_PLAIN = ["x_prompt", "x_sample", "cache_diff_k", "cache_diff_v", "cache_win_k", "cache_win_v", "c", "c_ctx", "ada_w",
          "ada_b", "norm_mix", "norm_ffn", "even_w_in", "even_w_out", "s5_log_step", "s5_d", "s5_w_glu", "diff_q_norm",
          "diff_k_norm", "diff_lambda", "diff_sub_norm", "odd_w_in", "odd_w_out", "win_q_norm", "win_k_norm",
          "win_sink", "pool_w", "pool_scale", "peer_w_q", "peer_u", "peer_v"]


def kernel(**inputs):
    import numpy as _np
    import concourse.bacc as _bacc
    from concourse import mybir as _mybir
    from concourse.bass_utils import run_bass_kernel_spmd as _run

    nc = _bacc.Bacc("TRN2", target_bir_lowering=False, num_devices=1)
    host = {name: _np.asarray(inputs[name]) for name in _PLAIN}
    lam = [_np.asarray(inputs[n])[0].transpose(0, 2, 1).reshape(128, 1, 32) for n in ("s5_lam_re", "s5_lam_im")]
    host["s5_lam"] = _np.concatenate(lam, axis=1)
    b = [_np.asarray(inputs[n])[0].transpose(0, 2, 1, 3).reshape(128, 1, 32, 16) for n in ("s5_b_re", "s5_b_im")]
    host["s5_b"] = _np.concatenate(b, axis=1)
    c = [_np.asarray(inputs[n])[0].transpose(0, 3, 1, 2).reshape(128, 1, 32, 16) for n in ("s5_c_re", "s5_c_im")]
    host["s5_c"] = _np.concatenate(c, axis=1)
    host["state_s5"] = _np.asarray(inputs["state_s5"])[0, 0].transpose(0, 3, 1, 2).reshape(128, 2, 32)
    host["peer_sub_keys"] = _np.asarray(inputs["peer_sub_keys"]).transpose(0, 4, 1, 2, 3).reshape(2, 128, 16, 128)
    host["consts"], host["pool_bands"] = constants()

    arrays, ins, outs = {}, {}, {}
    for name, a in host.items():
        a = _np.ascontiguousarray(a)
        arrays[f"in_{name}_dram"] = a
        ins[name] = nc.dram_tensor(f"in_{name}_dram", a.shape, _mybir.dt.from_np(a.dtype), kind="ExternalInput").ap()
    for name, shape in _OUTS:
        outs[name] = nc.dram_tensor(f"out_{name}_dram", shape, _mybir.dt.float32, kind="ExternalOutput").ap()
    build(nc, ins, outs)
    r = _run(nc, [arrays], core_ids=[0])
    return tuple(r.results[0][f"out_{name}_dram"] for name, _ in _OUTS)
```
